# Optimizing a Trainium2 kernel written in Bass

```python
import math
import jax, jax.numpy as jnp
from jax import lax
import numpy as np

D_MODEL = 1024
BATCH = 1
SEQ = 256
DEPTH = 2
DEC_BATCH = 8
DEC_SEQ = 4
PAST_LEN = 2048
PAGE_SIZE = 128

A_WIDTH = D_MODEL
A_GROUPS = 8
A_GROUP_DIM = A_WIDTH // A_GROUPS
A_CHUNK = 128
R_HEADS = 4
R_QK_DIM = D_MODEL // R_HEADS
R_V_DIM = 2 * R_QK_DIM
R_QK_WIDTH = R_HEADS * R_QK_DIM
R_V_WIDTH = R_HEADS * R_V_DIM
R_CHUNK = 128
ROPE_BASE = 10000.0
IN_COLS = 2 * A_WIDTH + 2 * R_QK_WIDTH + 2 * R_V_WIDTH + 2 * D_MODEL
N_GROUPS = 4
EXPERTS_PER_GROUP = 8
N_EXPERTS = N_GROUPS * EXPERTS_PER_GROUP
TOP_K = 2
EXPERT_DIM = 256
EPS = 1e-6

kernel_name = "hybrid_gmlp_retention_hmoe_decode_step"

def rmsnorm(x, g):
    xf = x.astype(jnp.float32)
    y = xf * lax.rsqrt(jnp.mean(xf * xf, axis=-1, keepdims=True) + EPS)
    return (y * g.astype(jnp.float32)).astype(x.dtype)

def layernorm(x, g, b):
    xf = x.astype(jnp.float32)
    mu = jnp.mean(xf, axis=-1, keepdims=True)
    var = jnp.mean(jnp.square(xf - mu), axis=-1, keepdims=True)
    y = (xf - mu) * lax.rsqrt(var + EPS) * g.astype(jnp.float32) + b.astype(jnp.float32)
    return y.astype(x.dtype)

def head_groupnorm(y):
    mu = jnp.mean(y, axis=-1, keepdims=True)
    var = jnp.mean(jnp.square(y - mu), axis=-1, keepdims=True)
    return (y - mu) * lax.rsqrt(var + EPS)

def rotary(x, pos):
    half = x.shape[-1] // 2
    inv_freq = jnp.power(ROPE_BASE, -jnp.arange(half, dtype=jnp.float32) / half)
    ang = pos.astype(jnp.float32)[:, None] * inv_freq[None, :]
    cos = jnp.cos(ang)[None, :, None, :]
    sin = jnp.sin(ang)[None, :, None, :]
    xf = x.astype(jnp.float32)
    x1, x2 = xf[..., :half], xf[..., half:]
    return jnp.concatenate([x1 * cos - x2 * sin, x1 * sin + x2 * cos], axis=-1)

def chunk_spatial_gating(u, v, w_s, b_s):
    B, T, _ = v.shape
    t_pad = -(-T // A_CHUNK) * A_CHUNK
    vp = jnp.pad(v, ((0, 0), (0, t_pad - T), (0, 0)))
    n = t_pad // A_CHUNK
    vg = vp.reshape(B, n, A_CHUNK, A_GROUPS, A_GROUP_DIM)
    causal = jnp.tril(jnp.ones((A_CHUNK, A_CHUNK), dtype=bool))
    ws = jnp.where(causal[None], w_s, jnp.zeros_like(w_s))
    mixed = jnp.einsum("gts,bnsgc->bntgc", ws, vg) + b_s.T[None, None, :, :, None]
    mixed = mixed.reshape(B, t_pad, A_WIDTH)[:, :T]
    return u * mixed

def retention(q, k, v, r0, chunk):
    B, T, H, dk = q.shape
    dv = v.shape[-1]
    n = T // chunk
    log_g = jnp.log1p(-jnp.power(2.0, -5.0 - jnp.arange(H, dtype=jnp.float32)))
    idx = jnp.arange(chunk, dtype=jnp.float32)
    diff = idx[:, None] - idx[None, :]
    decay_mask = jnp.where(diff >= 0, jnp.exp(log_g[:, None, None] * jnp.maximum(diff, 0.0)), 0.0)
    xi = jnp.exp(log_g[:, None] * (idx + 1.0))
    zeta = jnp.exp(log_g[:, None] * (chunk - 1.0 - idx))
    chunk_decay = jnp.exp(log_g * chunk)

    def to_chunks(a):
        return a.astype(jnp.float32).reshape(B, n, chunk, H, a.shape[-1]).transpose(1, 0, 3, 2, 4)

    qc, kc, vc = to_chunks(q), to_chunks(k), to_chunks(v)

    def step(r, inp):
        qi, ki, vi = inp
        scores = jnp.einsum("bhtd,bhsd->bhts", qi, ki) * decay_mask[None]
        inner = jnp.einsum("bhts,bhse->bhte", scores, vi)
        cross = jnp.einsum("bhtd,bhde->bhte", qi, r) * xi[None, :, :, None]
        r_new = r * chunk_decay[None, :, None, None] + jnp.einsum("bhsd,bhse->bhde", ki * zeta[None, :, :, None], vi)
        return r_new, inner + cross

    r_final, out = lax.scan(step, r0.astype(jnp.float32), (qc, kc, vc))
    out = out.transpose(1, 0, 3, 2, 4).reshape(B, T, H, dv)
    return out, r_final

def token_mixing(h, pos, r0, p, l):
    B, T, _ = h.shape
    z = h @ p["w_in"][l]
    sizes = [A_WIDTH, A_WIDTH, R_QK_WIDTH, R_QK_WIDTH, R_V_WIDTH, R_V_WIDTH, D_MODEL, D_MODEL]
    u, v, q, k, vr, gr, ga, gb = jnp.split(z, np.cumsum(sizes)[:-1].tolist(), axis=-1)
    u = jax.nn.gelu(u)
    v = layernorm(jax.nn.gelu(v), p["ln_v_g"][l], p["ln_v_b"][l])
    a = chunk_spatial_gating(u, v, p["w_s"][l], p["b_s"][l])
    q = rotary(q.reshape(B, T, R_HEADS, R_QK_DIM), pos)
    k = rotary(k.reshape(B, T, R_HEADS, R_QK_DIM), pos) * (R_QK_DIM ** -0.5)
    vr = vr.reshape(B, T, R_HEADS, R_V_DIM)
    chunk = R_CHUNK if T % R_CHUNK == 0 else T
    y, r_new = retention(q, k, vr, r0, chunk)
    y = head_groupnorm(y).reshape(B, T, R_V_WIDTH).astype(h.dtype)
    b = jax.nn.silu(gr) * y
    merged = jax.nn.sigmoid(ga) * (a @ p["w_a_out"][l]) + jax.nn.sigmoid(gb) * (b @ p["w_b_out"][l])
    return merged @ p["w_o"][l], r_new.astype(r0.dtype), v

def hier_moe(h, p, l):
    B, T, D = h.shape
    N = B * T
    x = h.reshape(N, D)
    g_logits = (x @ p["w_router_group"][l] + p["b_router_group"][l]).astype(jnp.float32)
    g_prob = jax.nn.softmax(g_logits, axis=-1)
    g_w, g_idx = lax.top_k(g_prob, 1)
    e_logits = (x @ p["w_router_expert"][l] + p["b_router_expert"][l]).astype(jnp.float32)
    e_logits = e_logits.reshape(N, N_GROUPS, EXPERTS_PER_GROUP)
    sel = jnp.broadcast_to(g_idx[:, :, None], (N, 1, EXPERTS_PER_GROUP))
    e_in = jnp.take_along_axis(e_logits, sel, axis=1)[:, 0]
    e_val, e_idx = lax.top_k(e_in, TOP_K)
    e_w = jax.nn.softmax(e_val, axis=-1) * g_w
    expert_id = g_idx * EXPERTS_PER_GROUP + e_idx
    combine = jnp.sum(jax.nn.one_hot(expert_id, N_EXPERTS, dtype=jnp.float32) * e_w[..., None], axis=1)
    gate = jnp.einsum("nd,edf->nef", x, p["w_gate"][l])
    up = jnp.einsum("nd,edf->nef", x, p["w_up"][l])
    hid = jax.nn.silu(gate) * up * combine[..., None].astype(x.dtype)
    out = jnp.einsum("nef,efd->nd", hid, p["w_down"][l])
    return out.reshape(B, T, D)

def run_trunk(x, c, pos, r_init, p):
    r_out, v_out = [], []
    silu_c = jax.nn.silu(c)
    for l in range(DEPTH):
        mod = silu_c @ p["w_mod"][l] + p["b_mod"][l]
        sh1, sc1, gt1, sh2, sc2, gt2 = jnp.split(mod[:, None, :], 6, axis=-1)
        h = rmsnorm(x, p["norm1_g"][l]) * (1.0 + sc1) + sh1
        if r_init is None:
            r0 = jnp.zeros((x.shape[0], R_HEADS, R_QK_DIM, R_V_DIM), jnp.float32)
        else:
            r0 = r_init[l]
        mix, r_new, v_rows = token_mixing(h, pos, r0, p, l)
        x = x + gt1 * mix
        h = rmsnorm(x, p["norm2_g"][l]) * (1.0 + sc2) + sh2
        x = x + gt2 * hier_moe(h, p, l)
        r_out.append(r_new)
        v_out.append(v_rows)
    return rmsnorm(x, p["final_g"]), jnp.stack(r_out), jnp.stack(v_out)

def setup_inputs(seed: int = 0) -> dict:
    key = jax.random.key(seed)
    ks = jax.random.split(key, 24)
    nrm = jax.random.normal
    D = D_MODEL
    f32 = jnp.float32
    return {
        "x_prompt": nrm(ks[0], (BATCH, SEQ, D), f32),
        "x_sample": nrm(ks[1], (DEC_BATCH, DEC_SEQ, D), f32),
        "state_ret": 0.05 * nrm(ks[2], (DEPTH, DEC_BATCH, R_HEADS, R_QK_DIM, R_V_DIM), f32),
        "c_prompt": nrm(ks[3], (BATCH, D), f32),
        "c_sample": nrm(ks[4], (DEC_BATCH, D), f32),
        "w_mod": 0.5 * D ** -0.5 * nrm(ks[5], (DEPTH, D, 6 * D), f32),
        "b_mod": 0.02 * nrm(ks[6], (DEPTH, 6 * D), f32),
        "norm1_g": 1.0 + 0.02 * nrm(ks[7], (DEPTH, D), f32),
        "w_in": D ** -0.5 * nrm(ks[8], (DEPTH, D, IN_COLS), f32),
        "ln_v_g": 1.0 + 0.02 * nrm(ks[9], (DEPTH, A_WIDTH), f32),
        "ln_v_b": 0.02 * nrm(ks[10], (DEPTH, A_WIDTH), f32),
        "w_s": A_CHUNK ** -0.5 * nrm(ks[11], (DEPTH, A_GROUPS, A_CHUNK, A_CHUNK), f32),
        "b_s": 1.0 + 0.02 * nrm(ks[12], (DEPTH, A_GROUPS, A_CHUNK), f32),
        "w_a_out": A_WIDTH ** -0.5 * nrm(ks[13], (DEPTH, A_WIDTH, D), f32),
        "w_b_out": R_V_WIDTH ** -0.5 * nrm(ks[14], (DEPTH, R_V_WIDTH, D), f32),
        "w_o": D ** -0.5 * nrm(ks[15], (DEPTH, D, D), f32),
        "norm2_g": 1.0 + 0.02 * nrm(ks[16], (DEPTH, D), f32),
        "w_router_group": D ** -0.5 * nrm(ks[17], (DEPTH, D, N_GROUPS), f32),
        "b_router_group": 0.01 * nrm(ks[18], (DEPTH, N_GROUPS), f32),
        "w_router_expert": D ** -0.5 * nrm(ks[19], (DEPTH, D, N_EXPERTS), f32),
        "b_router_expert": 0.01 * nrm(ks[20], (DEPTH, N_EXPERTS), f32),
        "w_gate": D ** -0.5 * nrm(ks[21], (DEPTH, N_EXPERTS, D, EXPERT_DIM), f32),
        "w_up": D ** -0.5 * nrm(ks[22], (DEPTH, N_EXPERTS, D, EXPERT_DIM), f32),
        "w_down": EXPERT_DIM ** -0.5 * nrm(ks[23], (DEPTH, N_EXPERTS, EXPERT_DIM, D), f32),
        "final_g": 1.0 + 0.02 * nrm(jax.random.fold_in(key, 99), (D,), f32),
    }

def reference(x_prompt, x_sample, state_ret, c_prompt, c_sample, w_mod, b_mod, norm1_g, w_in,
              ln_v_g, ln_v_b, w_s, b_s, w_a_out, w_b_out, w_o, norm2_g, w_router_group,
              b_router_group, w_router_expert, b_router_expert, w_gate, w_up, w_down, final_g):
    p = dict(w_mod=w_mod, b_mod=b_mod, norm1_g=norm1_g, w_in=w_in, ln_v_g=ln_v_g, ln_v_b=ln_v_b,
             w_s=w_s, b_s=b_s, w_a_out=w_a_out, w_b_out=w_b_out, w_o=w_o, norm2_g=norm2_g,
             w_router_group=w_router_group, b_router_group=b_router_group,
             w_router_expert=w_router_expert, b_router_expert=b_router_expert,
             w_gate=w_gate, w_up=w_up, w_down=w_down, final_g=final_g)
    pos_prompt = jnp.arange(x_prompt.shape[1], dtype=jnp.int32)
    pos_sample = PAST_LEN + jnp.arange(x_sample.shape[1], dtype=jnp.int32)
    y_prompt, state_ret_prompt, _ = run_trunk(x_prompt, c_prompt, pos_prompt, None, p)
    y_sample, state_ret_sample, state_chunk_v_sample = run_trunk(x_sample, c_sample, pos_sample, state_ret, p)
    return (y_prompt, y_sample, state_ret_prompt, state_ret_sample, state_chunk_v_sample)


_drawn_inputs = setup_inputs


def setup_inputs(seed=0):
    import zlib

    import numpy as np

    out = dict(_drawn_inputs(seed))
    spreads = {}
    factors = {'ln_v_g': 2.761,
     'ln_v_b': 2.86,
     'b_s': 7.474,
     'norm2_g': 3.329,
     'b_router_group': 8.0,
     'b_router_expert': 6.963,
     'final_g': 2.856}
    for name, (base, spread) in spreads.items():
        noise = np.random.default_rng([zlib.crc32(name.encode()), seed]).standard_normal(out[name].shape)
        drawn = base * np.exp(spread * noise) if base else spread * noise
        out[name] = __import__('jax').numpy.asarray(drawn.astype(out[name].dtype))
    for name, factor in factors.items():
        out[name] = (out[name] * factor).astype(out[name].dtype)
    return out
```

```python
import math
from contextlib import ExitStack

import numpy as np

import concourse.bass as bass
from concourse import mybir

D = 1024
SEQ = 256
DEPTH = 2
NB, NT = 8, 4
NS = NB * NT
TOK = SEQ + NS
PAST = 2048
P = 128
KT = D // P
HEADS, DK, DV = 4, 256, 512
QKW, VW = HEADS * DK, HEADS * DV
GROUPS, PER_GROUP, FE = 4, 8, 256
NE = GROUPS * PER_GROUP
ROWS = 1 + NB
EPS = 1e-6
SLOT = 4096
RING = 4
CAP = 32
OCAP = 128
NOVER = (2 * TOK) // (CAP + 1)

STEPS = (
    [("mod", 0), ("mod", 1), ("mod", 2), ("mod", 3), ("modflush", 3), ("norm", 1)]
    + [("v", 0), ("v", 1), ("u", 0), ("lnfold", 0), ("u", 1), ("lnfold", 1)]
    + [("mix", i) for i in range(4)] + [("mixs", j) for j in range(4)]
    + [("ga", 0), ("ga", 1), ("a", 0), ("a", 1), ("q", 0), ("q", 1), ("k", 0), ("k", 1)]
    + [("vr", i) for i in range(4)] + [("gr", 0), ("gr", 1), ("kts", 0), ("scs", 0), ("kt", 0), ("sc", 0), ("gr", 2)]
    + [("st", 0), ("gr", 3), ("st", 1), ("r1", 0), ("mod", 4), ("y", 0), ("st", 2), ("kt", 1), ("sc", 1),
       ("mod", 5), ("st", 3), ("r1", 1), ("mod", 6), ("y", 1), ("st", 4), ("kt", 2), ("sc", 2), ("mod", 7),
       ("st", 5), ("r1", 2), ("mod", 8), ("y", 2), ("st", 6), ("kt", 3), ("sc", 3), ("mod", 9),
       ("st", 7), ("r1", 3), ("modflush", 9), ("y", 3), ("ysum", 0)]
    + [("gb", 0), ("gb", 1), ("bts", 0)] + [("bt", i) for i in range(8)]
    + [("b", i) for i in range(4)] + [("o", 0), ("o", 1)]
    + [("norm", 2), ("mod", 10), ("mod", 11), ("modflush", 11), ("route", 0)]
)
SLOT_KINDS = ("mod", "v", "u", "ga", "a", "q", "k", "vr", "gr", "st", "gb", "b", "o")
SLOT_STEPS = [s for s in STEPS if s[0] in SLOT_KINDS]
SLOT_OF = {s: n for n, s in enumerate(SLOT_STEPS)}
TOKEN_SLOTS = len(SLOT_STEPS)
MOE_SLOTS = NE // 2 * 3
LAYER_SLOTS = TOKEN_SLOTS + MOE_SLOTS
assert TOKEN_SLOTS % RING == 0 and MOE_SLOTS % (3 * RING) == 0

YBANK = 7


def tiles_of(step):
    kind, i = step
    if kind == "mod":
        return ["modp"] + (["modt"] if i not in (0, 4, 10) else [])
    if kind == "modflush":
        return ["modt"]
    if kind == "norm":
        return ["ss"]
    if kind in ("v", "vr", "gr"):
        return ["p0", "p1", "s"]
    if kind in ("u", "ga", "a", "q", "k", "gb", "o"):
        return ["c0", "c1", "c2", "c3"]
    if kind == "b":
        return ["c0", "c1"]
    if kind == "st":
        return [f"{dt}{h}" for dt in range(2) for h in range(HEADS)]
    if kind == "r1":
        return ["r0", "r1", "y0"]
    if kind == "y":
        return ["y1", "f0", "f1"]
    if kind == "ysum":
        return []
    if kind == "route":
        return ["lg", "lgt"] + [f"h{j}" for j in range(6)] + ["rk", "cnt", "ob", "bc0", "bc1", "bc2"]
    return ["t"]


TILE_NAMES = [(s, t) for s in STEPS for t in tiles_of(s)]
TILES, used = {}, [0] * 8
for n, name in enumerate(TILE_NAMES):
    TILES[name] = (n % 7, used[n % 7])
    used[n % 7] += 1
TILES["ysample"] = (YBANK, used[YBANK])
used[YBANK] += 1
for n, name in enumerate(("gather0", "gather1")):
    TILES[name] = (n, used[n])
    used[n] += 1
TOKEN_USES = list(used)
MOE_TILES, used = {}, [0] * 8
for g in range(2):
    for name, bank in (
        [("gu0", 2), ("ga", 0), ("h0", 6), ("gu1", 3), ("gb", 1), ("h1", 6), ("y0", 4), ("y1", 5)]
        + [(f"c{ft}", 7 - ft % 2) for ft in range(KT)]
    ):
        MOE_TILES[g, name] = (bank, used[bank])
        used[bank] += 1
BODY_USES = list(used)
BODIES = NE // 8
FINAL_BANK = 0
LAYER_USES = [TOKEN_USES[b] + BODIES * BODY_USES[b] for b in range(8)]

CONSTS = {}
_at = 0
for _name, _width in [
    ("ident", P), ("tri", P), ("tri_incl", P), ("fold", P), ("cos", TOK), ("sin", TOK),
    ("decay", HEADS * P), ("xi", HEADS * P), ("xis", 2 * HEADS * NS), ("masks", P), ("mixmask", NS),
    ("zeta", HEADS), ("zetas", NB), ("iota", P), ("iota4", 4), ("iota8", 8), ("iota32", NE),
    ("base32", NE), ("slotcol", 1), ("eps", 1), ("half", 1), ("sel", P), ("novr", NOVER), ("gurow", NE),
    ("drow", NE), ("dhalf", NE),
]:
    CONSTS[_name] = (_at, _width)
    _at += _width
CW = _at
PARAMS = {}
_at = 0
for _name, _width in [
    ("bmod", 6 * KT), ("g1", KT), ("g2", KT), ("lng", D), ("lnb", D), ("lngs", 2 * P), ("lnbs", 2 * P),
    ("bs", 8 * P), ("wst", 8 * P), ("bss", 8 * NS), ("wss", 2 * NS), ("wr", KT * 36), ("br", 1),
]:
    PARAMS[_name] = (_at, _width)
    _at += _width
PW = _at


def decay(head):
    return math.log1p(-(2.0 ** (-5 - head)))


def constants():
    f = np.float32
    c = np.zeros((P, CW), f)

    def put(name, value):
        at, width = CONSTS[name]
        c[:, at:at + width] = np.asarray(value, f).reshape(P, width)

    p = np.arange(P)
    put("ident", np.eye(P))
    put("tri", p[:, None] < p[None, :])
    put("tri_incl", p[:, None] <= p[None, :])
    put("fold", (p[:, None] % NS == p[None, :] % NS) * 0.25)
    half = DK // 2
    inv_freq = np.power(f(10000.0), -np.arange(half, dtype=f) / f(half)).astype(f)
    pos = np.concatenate([np.arange(SEQ), np.tile(PAST + np.arange(NT), NB)]).astype(f)
    angle = (inv_freq[:, None] * pos[None, :]).astype(f)
    put("cos", np.cos(angle))
    put("sin", np.sin(angle))
    g = np.array([decay(h) for h in range(HEADS)])
    d = p[None, :] - p[:, None]
    scale = DK ** -0.5
    dec = np.where(d[:, None, :] >= 0, np.exp(g[None, :, None] * np.maximum(d, 0)[:, None, :]), 0.0) * scale
    put("decay", dec)
    put("xi", np.broadcast_to(np.exp(g[:, None] * (p + 1.0)), (P, HEADS, P)))
    t4 = np.arange(NT)
    xis = np.broadcast_to(np.exp(g[:, None] * (t4 + 1.0))[None, :, None, None, :], (P, HEADS, 2, NB, NT))
    put("xis", xis)
    h, b, s = p // NS, p % NS // NT, p % NT
    same = (h[:, None] == h[None, :]) & (b[:, None] == b[None, :]) & (s[None, :] >= s[:, None])
    put("masks", np.where(same, np.exp(g[h][:, None] * np.maximum(s[None, :] - s[:, None], 0)), 0.0) * scale)
    put("mixmask", same[:NS, :NS][p % NS])
    put("zeta", np.exp(g[None, :] * (P - 1.0 - p[:, None])) * scale)
    put("zetas", (b[:, None] == np.arange(NB)[None, :]) * np.exp(g[h] * (NT - 1.0 - s))[:, None] * scale)
    put("iota", np.broadcast_to(p, (P, P)))
    put("iota4", np.broadcast_to(np.arange(4) - 64, (P, 4)))
    put("iota8", np.broadcast_to(np.arange(8) - 64, (P, 8)))
    e = np.arange(NE)
    put("iota32", np.broadcast_to(e - 576, (P, NE)))
    put("base32", np.broadcast_to(e * CAP, (P, NE)))
    put("slotcol", p)
    put("eps", np.full(P, EPS))
    put("half", np.full(P, -0.5))
    f2, s2 = np.arange(2), np.arange(NS)
    sel = (h[:, None, None, None] == 2 * f2[None, None, :, None] + f2[None, :, None, None])
    put("sel", sel & ((p % NS)[:, None, None, None] == s2))
    put("novr", np.broadcast_to(np.arange(NOVER), (P, NOVER)))
    put("gurow", np.broadcast_to(TOKEN_SLOTS + e // 2 * 3 + e % 2, (P, NE)))
    put("drow", np.broadcast_to(TOKEN_SLOTS + e // 2 * 3 + 2, (P, NE)))
    put("dhalf", np.broadcast_to(e % 2, (P, NE)))
    return c


QK_AT = 0
MERGED_AT = QK_AT + 2 * KT * TOK
VV_AT = MERGED_AT + KT * TOK
SG_AT = VV_AT + 2 * VW + DV
WORK = SG_AT + 2 * VW + DV
TURNS = 6
SUM_BANKS = (6, 7, 2, 3, 4, 5)
VARS = 3 + 2 * HEADS + 1
LN_DONE = 3
B_DONE = 2 * HEADS + 1
GROUPS4 = NE // 4
SELS = GROUPS4 + 2
SAMPLES = slice(SEQ, TOK)
TTILES = ((0, P), (1, P), (2, NS))


def build(nc, stream, consts, params, x_in, c_in, gfin, y_out, state_out, state_sample_out, v_out):
    f32, i32 = mybir.dt.float32, mybir.dt.int32
    ALU, ACT, AX = mybir.AluOpType, mybir.ActivationFunctionType, mybir.AxisListType
    with ExitStack() as ctx:
        def sb(name, shape, dt=f32):
            return ctx.enter_context(nc.sbuf_tensor(name, shape, dt))

        def sem(name):
            return ctx.enter_context(nc.semaphore(name))

        ring = [sb(f"ring{r}", [P, SLOT]) for r in range(RING)]
        cst = sb("cst", [P, CW])
        prm = sb("prm", [P, PW])
        xT = sb("xT", [P, KT, TOK])
        hT = sb("hT", [P, KT, TOK])
        cT = sb("cT", [P, KT, 32])
        mod = sb("mod", [P, 6 * KT, ROWS])
        scaled = sb("scaled", [P, KT, ROWS])
        modp = sb("modp", [P, 2, 512])
        modsum = sb("modsum", [P, 4, ROWS])
        ones = sb("ones", [P, P])
        work = sb("work", [P, WORK])
        rope = sb("rope", [P, 2, TOK])
        rms = sb("rms", [P, TOK])
        stats = sb("stats", [P, 2, 6])
        moments = sb("moments", [P, 4, 2])
        rstd = sb("rstd", [P, 2])
        kz = sb("kz", [P, 2, DK])
        scT = sb("scT", [P, 2, P])
        qx = sb("qx", [P, 2, P])
        kzs = sb("kzs", [P, DK])
        kzm = sb("kzm", [P, 2, DK])
        scs = sb("scs", [P, P])
        novf = sb("novf", [1, 2])
        novi = sb("novi", [1, 2], i32)
        otab = sb("otab", [1, 3, NOVER], i32)
        gfs = sb("gfs", [P, KT])
        ovd = sb("ovd", [P, 2 * D])
        vals = sb("vals", [P, 3, 4])
        slotcol = sb("slotcol_now", [P, 1])
        ps = [ctx.enter_context(nc.psum_tensor(f"ps{b}", [P, 512], f32)) for b in range(8)]

        def C(name):
            at, width = CONSTS[name]
            return cst[:, at:at + width]

        def R(name):
            at, width = PARAMS[name]
            return prm[:, at:at + width]

        def cut(ap, *shape):
            if len(shape) == 1:
                return ap
            names = "abc"[:len(shape)]
            return ap.rearrange(f"p ({' '.join(names)}) -> p {' '.join(names)}", **dict(zip(names, shape)))

        def W(at, *shape):
            return cut(work[:, at:at + int(np.prod(shape))], *shape)

        qT = W(QK_AT, KT, TOK)
        kT = W(QK_AT + KT * TOK, KT, TOK)
        bT = W(QK_AT, 2 * KT, TOK)
        merged = W(MERGED_AT, KT, TOK)
        vn = W(VV_AT, 2, D)
        vns = W(VV_AT + 2 * D, 2, P)
        uT = W(VV_AT + 2 * D + 2 * P, KT, TOK)
        vr = W(VV_AT, 2, VW)
        vrs = W(VV_AT + 2 * VW, DV)
        sgb = W(VV_AT, KT, TOK)
        sg = W(SG_AT, 2, VW)
        sgs = W(SG_AT + 2 * VW, DV)
        square = W(SG_AT, KT, TOK)
        mixed = W(SG_AT, 512)
        ln_at, bs_at = PARAMS["lng"][0], PARAMS["bs"][0]
        qm = cut(prm[:, ln_at:ln_at + 2 * D], NB, KT, NS)
        r1 = cut(prm[:, bs_at:bs_at + 2 * D], 2, 2, DV)

        place = [0]

        def X(*shape):
            at = place[0]
            place[0] += int(np.prod(shape))
            return W(at, *shape)

        htok = X(3, D)
        hg = X(2, KT, P)
        psel = cut(X(6 * P), 6, P)
        pt = X(2, TOK)
        rows4 = X(4, TOK)
        hid = X(4, 64)
        hidT = X(4 * 2 * CAP)
        yslot = X(D)
        part = X(TOK)
        ovw = work[:, place[0]:place[0] + SLOT]
        diag = X(3 * 4, P)
        rt, prod, ein, e2, oh8, oh8b = X(3, 36), X(3, NE), X(3, 8), X(3, 8), X(3, 8), X(3, 8)
        g4, g4b, eg, col = X(3, 4), X(3, 4), X(3, 4), X(16, 3)
        oh1, oh2, cnt, slots, picked = X(3, NE), X(3, NE), X(3, NE), X(3, NE), X(3, NE)
        diff, nbb, ot1, ot2, otf, obe, lgs = X(NE), X(P), X(NOVER, NE), X(NOVER, NE), X(3, NOVER), X(2, NE), X(TOK)
        assert place[0] <= WORK
        assert ovw.shape[1] == SLOT

        slot_loaded = [sem(f"slot_loaded{r}") for r in range(RING)]
        slot_free = [sem(f"slot_free{r}") for r in range(RING)]
        acc_ready = [sem(f"acc_ready{b}") for b in range(8)]
        acc_free = [sem(f"acc_free{b}") for b in range(8)]
        consts_loaded = sem("consts_loaded")
        params_loaded = sem("params_loaded")
        setup_done = sem("setup_done")
        silu_c_ready = sem("silu_c_ready")
        square_ready = sem("square_ready")
        rms_ready = sem("rms_ready")
        scaled_ready = sem("scaled_ready")
        affine_ready = sem("affine_ready")
        samples_ready = sem("samples_ready")
        var_ready = sem("var_ready")
        rstd_ready = sem("rstd_ready")
        ln_ready = sem("ln_ready")
        fold_ready = sem("fold_ready")
        v_stored = sem("v_stored")
        mask_ready = sem("mask_ready")
        qm_zero = sem("qm_zero")
        qm_ready = sem("qm_ready")
        qx_ready = sem("qx_ready")
        kzm_ready = sem("kzm_ready")
        rf_stored = sem("rf_stored")
        b_ready = sem("b_ready")
        x_ready = sem("x_ready")
        exp_in = sem("exp_in")
        exp_out = sem("exp_out")
        counts_ready = sem("counts_ready")
        tables_ready = sem("tables_ready")
        sel_ready = sem("sel_ready")
        pt_ready = sem("pt_ready")
        silu_ready = sem("silu_ready")
        over_gu_loaded = sem("over_gu_loaded")
        over_down_loaded = sem("over_down_loaded")
        over_gu_made = sem("over_gu_made")
        over_hidden = sem("over_hidden")
        over_down_made = sem("over_down_made")
        over_sum_made = sem("over_sum_made")
        over_sum_taken = sem("over_sum_taken")
        over_gather_made = sem("over_gather_made")
        over_rows_ready = sem("over_rows_ready")
        over_sel_ready = sem("over_sel_ready")
        y_stored = sem("y_stored")

        def bank(name):
            return TILES[name][0]

        def count(name, l):
            b, u = TILES[name]
            return l * LAYER_USES[b] + (u + 1)

        def mbank(name):
            return MOE_TILES[name][0]

        def mcount(name, l, i, back=0):
            b, u = MOE_TILES[name]
            return l * LAYER_USES[b] + i * BODY_USES[b] + (TOKEN_USES[b] + u + 1 - back * BODY_USES[b])

        PER_RING = 16 * LAYER_SLOTS // RING

        def wait_reads(eng, names, l, free=None):
            least = {}
            for name in names:
                b, u = TILES[name]
                least[b] = max(least.get(b, 0), u + 2)
            if free is not None:
                b, u = TILES[free]
                least[b] = max(least.get(b, 0), u + 1)
            for b, value in least.items():
                eng.wait_ge(acc_free[b], l * LAYER_USES[b] + value)

        def wait_free(pe, name, l, reads=()):
            wait_reads(pe, reads, l, free=name)
            return ps[bank(name)]

        def wait_made(eng, name, l):
            eng.wait_ge(acc_ready[bank(name)], count(name, l))
            return ps[bank(name)]

        def wait_read(eng, name, l):
            wait_reads(eng, [name], l)

        def mwait_free(pe, name, l, i):
            pe.wait_ge(acc_free[mbank(name)], mcount(name, l, i))
            return ps[mbank(name)]

        def mwait_made(eng, name, l, i, back=0):
            eng.wait_ge(acc_ready[mbank(name)], mcount(name, l, i, back))
            return ps[mbank(name)]

        def mwait_read(eng, name, l, i):
            eng.wait_ge(acc_free[mbank(name)], mcount(name, l, i) + 1)

        def made(ins, name):
            ins.then_inc(acc_ready[bank(name)], 1)

        def mmade(ins, name):
            ins.then_inc(acc_ready[mbank(name)], 1)

        def taken(ins, name):
            ins.then_inc(acc_free[bank(name)], 1)

        def mtaken(ins, name):
            ins.then_inc(acc_free[mbank(name)], 1)

        def row(ap, index):
            return ap[bass.ds(index, 1), :, :].rearrange("o p w -> (o p) w")

        block = ctx.enter_context(nc.Block())

        @block.sync
        def _(sp):
            with sp.Fori(0, DEPTH * LAYER_SLOTS // RING) as n:
                for r in range(RING):
                    sp.wait_ge(slot_free[r], n * 16 + 16)
                    sp.dma_start(ring[r][:, :], row(stream, n * RING + r)).then_inc(slot_loaded[r], 16)

        @block.gpsimd
        def _(pool):
            for r in range(RING):
                pool.sem_inc(slot_free[r], 16)
            pool.dma_start(cst[:, :], consts).then_inc(consts_loaded, 16)
            pool.dma_start(xT[:, :, :], x_in).then_inc(consts_loaded, 16)
            pool.dma_start(cT[:, :, :], c_in).then_inc(consts_loaded, 16)
            pool.dma_start(gfs[:, :], gfin).then_inc(consts_loaded, 16)
            pool.dma_start(prm[:, :], params[0, :, :]).then_inc(params_loaded, 16)
            pool.memset(ones[:, :], 1.0).then_inc(setup_done, 1)
            pool.memset(novf[:, :], 0.0).then_inc(setup_done, 1)
            pool.wait_ge(consts_loaded, 64)

            def inverse_root(l, n):
                pool.wait_ge(var_ready, l * VARS + n + 1)
                if n >= 5:
                    pool.wait_ge(b_ready, l * B_DONE + n - 4)
                m = n % 2
                pool.tensor_tensor(rstd[:, m:m + 1], moments[:, m, 1:2], C("eps"), ALU.add)
                pool.drain()
                pool.tensor_tensor(rstd[:, m:m + 1], rstd[:, m:m + 1], C("half"), ALU.pow).then_inc(rstd_ready, 1)

            with pool.Fori(0, DEPTH) as l:
                pool.wait_ge(params_loaded, l * 16 + 16)
                wss = cut(R("wss"), 2, NS)
                mask = C("mixmask").rearrange("p (o t) -> p o t", o=1).broadcast_to([P, 2, NS])
                pool.tensor_tensor(wss, wss, mask, ALU.mult).then_inc(mask_ready, 1)
                wst = cut(R("wst"), 8, P)
                pool.affine_select(out=wst, in_=wst, compare_op=ALU.is_ge, fill=0.0, base=0,
                                   pattern=[[0, 8], [1, P]], channel_multiplier=-1).then_inc(mask_ready, 1)
                n_var = 0
                for step in STEPS:
                    kind, i = step
                    if step == ("v", 1):
                        inverse_root(l, 0)
                        inverse_root(l, 1)
                        n_var = 2
                    elif step == ("lnfold", 1):
                        inverse_root(l, n_var)
                        n_var += 1
                        pool.wait_ge(ln_ready, l * LN_DONE + LN_DONE)
                        pool.dma_start(row(v_out, l), work[:, VV_AT + 2 * D:VV_AT + 2 * D + 2 * P]).then_inc(v_stored, 16)
                        pool.memset(prm[:, ln_at:ln_at + 2 * D], 0.0).then_inc(qm_zero, 1)
                    elif kind == "st":
                        if i == 0:
                            wait_read(pool, (("kts", 0), "t"), l)
                        if i >= 2:
                            wait_made(pool, (("st", i - 2), f"1{HEADS - 1}"), l)
                        pool.tensor_tensor(kzm[:, i % 2, :], kzs[:, :], C("zetas")[:, i:i + 1].broadcast_to([P, DK]), ALU.mult).then_inc(kzm_ready, 1)
                    elif kind == "r1":
                        inverse_root(l, n_var)
                        n_var += 1
                    elif kind == "y":
                        inverse_root(l, n_var)
                        n_var += 1
                        wait_reads(pool, [(step, f"f{f}") for f in range(2)], l)
                        pool.dma_start(row(state_out, l * HEADS + i), r1[:, i % 2, :, :].rearrange("p d e -> p (d e)")).then_inc(rf_stored, 16)
                    elif kind == "ysum":
                        inverse_root(l, n_var)
                        n_var += 1
                assert n_var == VARS
                pool.wait_ge(rf_stored, l * (16 * HEADS) + 16 * HEADS)
                wait_made(pool, (("route", 0), "bc2"), l)
                pool.wait_ge(tables_ready, l + 1)
                pool.dma_start(prm[:, :], row(params, l + 1)).then_inc(params_loaded, 16)
                first = pool.value_load(novi[0:1, 0:1], min_val=0, max_val=DEPTH * NOVER)
                number = pool.value_load(novi[0:1, 1:2], min_val=0, max_val=NOVER)
                with pool.If(number > 0):
                    with pool.Fori(0, number) as n:
                        o = first + n
                        gu = pool.value_load(otab[0:1, 0, bass.ds(n, 1)], min_val=0, max_val=LAYER_SLOTS - 1)
                        dn = pool.value_load(otab[0:1, 1, bass.ds(n, 1)], min_val=0, max_val=LAYER_SLOTS - 1)
                        half = pool.value_load(otab[0:1, 2, bass.ds(n, 1)], min_val=0, max_val=1)
                        halves = stream.rearrange("s p (q w) -> s q p w", q=2)
                        pool.wait_ge(over_gu_made, o + 1)
                        pool.dma_start(ovw, row(stream, l * LAYER_SLOTS + gu)).then_inc(over_gu_loaded, 16)
                        pool.wait_ge(over_down_made, o + 1)
                        pool.dma_start(ovd[:, :], halves[bass.ds(l * LAYER_SLOTS + dn, 1), bass.ds(half, 1), :, :].rearrange("s q p w -> (s q p) w")).then_inc(over_down_loaded, 16)
                pool.nop()
            pool.wait_ge(params_loaded, 16 * (DEPTH + 1))
            pool.wait_ge(v_stored, 16 * DEPTH)
            for r in range(RING):
                pool.wait_ge(slot_free[r], 16 * (DEPTH * LAYER_SLOTS // RING + 1))
            pool.wait_ge(x_ready, DEPTH * 2 + 1)
            pool.dma_start(y_out, hT[:, :, :]).then_inc(y_stored, 16)
            pool.wait_ge(y_stored, 16)

        @block.tensor
        def _(pe):
            freed = []

            def mm(out, lhsT, rhs, start, stop, **k):
                ins = nc.tensor.matmul(out, lhsT, rhs, start=start, stop=stop, **k)
                if freed:
                    ins.then_inc(slot_free[freed.pop()], 16)
                    return None
                return ins

            def transposed(out, in_, ident):
                return mm(out, in_, ident, True, True, is_transpose=True)

            def slot(step, l):
                n = SLOT_OF[step]
                pe.wait_ge(slot_loaded[n % RING], l * PER_RING + 16 * (n // RING + 1))
                return ring[n % RING]

            def mslot(n, l, i):
                pe.wait_ge(slot_loaded[n % RING], l * PER_RING + i * (16 * 12 // RING) + 16 * ((TOKEN_SLOTS + n) // RING + 1))
                return ring[n % RING]

            def feature_major(step, l, act, k_tiles=KT, cols=4, reads=()):
                w = cut(slot(step, l)[:, :], k_tiles, cols * P)
                for c in range(cols):
                    out = wait_free(pe, (step, f"c{c}"), l, reads if c == 0 else ())
                    for k in range(k_tiles):
                        last = mm(out[:, 0:TOK], w[:, k, c * P:c * P + P], act[:, k, :], k == 0, k == k_tiles - 1)
                    made(last, (step, f"c{c}"))
                freed.append(SLOT_OF[step] % RING)

            def token_major(step, l):
                w = cut(slot(step, l)[:, :], KT, 512)
                for tt in range(2):
                    out = wait_free(pe, (step, f"p{tt}"), l)
                    for k in range(KT):
                        last = mm(out[:, :], hT[:, k, tt * P:tt * P + P], w[:, k, :], k == 0, k == KT - 1)
                    made(last, (step, f"p{tt}"))
                out = wait_free(pe, (step, "s"), l)
                for k in range(KT):
                    for j in range(4):
                        last = mm(out[32 * j:32 * j + 32, 0:P], hT[:, k, SAMPLES], w[:, k, j * P:j * P + P],
                                  k == 0, k == KT - 1, skip_group_check=True)
                made(last, (step, "s"))
                freed.append(SLOT_OF[step] % RING)

            def mod_product(step, l):
                w = cut(slot(step, l)[:, :], KT, 512)
                out = wait_free(pe, (step, "modp"), l)
                for half in range(2):
                    for j in range(4):
                        last = mm(out[32 * j:32 * j + 32, :], cT[:, 2 * j + half, :], w[:, 2 * j + half, :],
                                  half == 0, half == 1, skip_group_check=True)
                made(last, (step, "modp"))
                freed.append(SLOT_OF[step] % RING)

            def mod_transpose(i, name, l):
                out = wait_free(pe, name, l, [(("mod", i), "modp")])
                for c in range(4):
                    last = transposed(out[:, c * P:c * P + P], modp[:, i % 2, c * P:c * P + P], C("ident"))
                made(last, name)

            def gather(out, half, buf):
                for kk in range(4):
                    k = 4 * half + kk
                    for tt, rows in TTILES:
                        last = mm(out[:, kk * P:kk * P + P], htok[0:rows, tt, k * P:k * P + P],
                                  psel[0:rows, 3 * buf + tt, :], tt == 0, tt == 2)
                return last

            pe.wait_ge(consts_loaded, 64)
            pe.wait_ge(setup_done, 2)
            pe.wait_ge(silu_c_ready, 1)
            with pe.Fori(0, DEPTH) as l:
                for step in STEPS:
                    kind, i = step
                    if kind == "mod":
                        mod_product(step, l)
                        if i not in (0, 4, 10):
                            mod_transpose(i - 1, (step, "modt"), l)
                    elif kind == "modflush":
                        mod_transpose(i, (step, "modt"), l)
                    elif kind == "norm":
                        out = wait_free(pe, (step, "ss"), l)
                        pe.wait_ge(square_ready, l * 2 + i)
                        for k in range(KT):
                            last = mm(out[:, 0:TOK], ones[:, :], square[:, k, :], k == 0, k == KT - 1)
                        made(last, (step, "ss"))
                        if i == 1:
                            pe.wait_ge(affine_ready, l * (2 * KT) + KT)
                            pe.wait_ge(samples_ready, l * 2 + 1)
                    elif kind in ("v", "vr", "gr"):
                        token_major(step, l)
                    elif kind in ("u", "ga", "q", "k", "gb"):
                        feature_major(step, l, hT)
                    elif kind == "a":
                        feature_major(step, l, uT, reads=[((m, n), "t") for m in ("mix", "mixs") for n in range(4)])
                    elif kind == "b":
                        feature_major(step, l, bT, 2 * KT, 2, reads=[(("bts", 0), "t")] + [(("bt", n), "t") for n in range(8)])
                    elif kind == "o":
                        feature_major(step, l, merged, reads=[(("b", n), f"c{c}") for n in range(4) for c in range(2)])
                    elif kind == "lnfold":
                        pe.wait_ge(fold_ready, l * 2 + i + 1)
                        out = wait_free(pe, (step, "t"), l)
                        for m in range(2):
                            last = mm(out[:, m:m + 1], C("fold"), moments[:, 2 + i, m:m + 1], True, True)
                        made(last, (step, "t"))
                    elif kind == "mix":
                        if i == 0:
                            pe.wait_ge(mask_ready, l * 2 + 2)
                            pe.wait_ge(ln_ready, l * LN_DONE + 2)
                        c = i // 2
                        out = wait_free(pe, (step, "t"), l)
                        for gg in range(4):
                            g = 4 * (i % 2) + gg
                            last = mm(out[:, gg * P:gg * P + P], vn[:, c, g * P:g * P + P], R("wst")[:, g * P:g * P + P], True, True)
                        made(last, (step, "t"))
                    elif kind == "mixs":
                        pe.wait_ge(ln_ready, l * LN_DONE + 3)
                        out = wait_free(pe, (step, "t"), l)
                        for s in range(2):
                            last = mm(out[:, s * NS:s * NS + NS], vns[32 * i:32 * i + 32, s, :],
                                      R("wss")[32 * i:32 * i + 32, s * NS:s * NS + NS], True, True)
                        made(last, (step, "t"))
                    elif kind == "kts":
                        out = wait_free(pe, (step, "t"), l, [((m, s), f"c{c}") for m in "qk" for s in range(2) for c in range(4)])
                        for dt in range(2):
                            for h in range(HEADS):
                                last = mm(out[32 * h:32 * h + 32, dt * P:dt * P + P], kT[:, 2 * h + dt, SAMPLES], C("ident"),
                                          True, True, skip_group_check=True)
                        made(last, (step, "t"))
                    elif kind == "scs":
                        out = wait_free(pe, (step, "t"), l)
                        for dt in range(2):
                            for h in range(HEADS):
                                last = mm(out[32 * h:32 * h + 32, 0:NS], kT[:, 2 * h + dt, SAMPLES], qT[:, 2 * h + dt, SAMPLES],
                                          dt == 0, dt == 1, skip_group_check=True)
                        made(last, (step, "t"))
                    elif kind == "kt":
                        out = wait_free(pe, (step, "t"), l)
                        for c in range(2):
                            for dt in range(2):
                                last = transposed(out[:, (2 * c + dt) * P:(2 * c + dt) * P + P], kT[:, 2 * i + dt, c * P:c * P + P], C("ident"))
                        made(last, (step, "t"))
                    elif kind == "sc":
                        out = wait_free(pe, (step, "t"), l)
                        for c in range(2):
                            for dt in range(2):
                                last = mm(out[:, c * P:c * P + P], kT[:, 2 * i + dt, c * P:c * P + P],
                                          qT[:, 2 * i + dt, c * P:c * P + P], dt == 0, dt == 1)
                        made(last, (step, "t"))
                    elif kind == "r1":
                        values = vr[:, 0, i * DV:i * DV + DV]
                        for dt in range(2):
                            out = wait_free(pe, (step, f"r{dt}"), l, [(("kt", i), "t")] + [(("vr", n), t) for n in range(4) for t in ("p0", "p1")])
                            made(mm(out[:, :], kz[:, 0, dt * P:dt * P + P], values, True, True), (step, f"r{dt}"))
                        out = wait_free(pe, (step, "y0"), l, [(("sc", i), "t")])
                        made(mm(out[:, :], scT[:, 0, :], values, True, True), (step, "y0"))
                    elif kind == "y":
                        values = vr[:, 1, i * DV:i * DV + DV]
                        out = wait_free(pe, (step, "y1"), l)
                        mm(out[:, :], scT[:, 1, :], values, True, False)
                        pe.wait_ge(qx_ready, l * HEADS + i + 1)
                        for dt in range(2):
                            wait_read(pe, (("r1", i), f"r{dt}"), l)
                            last = mm(out[:, :], qx[:, dt, :], r1[:, i % 2, dt, :], False, dt == 1)
                        made(last, (step, "y1"))
                        for dt in range(2):
                            out = wait_free(pe, (step, f"f{dt}"), l)
                            made(mm(out[:, :], kz[:, 1, dt * P:dt * P + P], values, True, True), (step, f"f{dt}"))
                    elif kind == "st":
                        out = ps[YBANK]
                        if i == 0:
                            wait_free(pe, "ysample", l, [(("scs", 0), "t")] + [(("vr", m), "s") for m in range(4)])
                            mm(out[:, :], scs[:, :], vrs, True, False, skip_group_check=True)
                            pe.wait_ge(qm_ready, l + 1)
                        state = cut(slot(step, l)[:, :], HEADS, 2, DV)
                        for dt in range(2):
                            for h in range(HEADS):
                                last = mm(out[32 * h:32 * h + 32, :], qm[:, i, 2 * h + dt, :], state[:, h, dt, :],
                                          False, i == NB - 1 and dt == 1, skip_group_check=True)
                        if i == NB - 1:
                            made(last, "ysample")
                        pe.wait_ge(kzm_ready, l * NB + i + 1)
                        for dt in range(2):
                            for h in range(HEADS):
                                wait_free(pe, (step, f"{dt}{h}"), l)
                            for h in range(HEADS):
                                name = (step, f"{dt}{h}")
                                made(mm(ps[bank(name)][:, :], kzm[32 * h:32 * h + 32, i % 2, dt * P:dt * P + P],
                                        vrs[32 * h:32 * h + 32, :], True, True), name)
                    elif kind == "bts":
                        pe.wait_ge(b_ready, l * B_DONE + B_DONE)
                        out = wait_free(pe, (step, "t"), l)
                        for c in range(4):
                            last = transposed(out[:, c * P:c * P + P], sgs[:, c * P:c * P + P], C("ident"))
                        made(last, (step, "t"))
                    elif kind == "bt":
                        out = wait_free(pe, (step, "t"), l)
                        tt, q = i // 4, i % 4
                        for c in range(4):
                            last = transposed(out[:, c * P:c * P + P], sg[:, tt, q * DV + c * P:q * DV + c * P + P], C("ident"))
                        made(last, (step, "t"))
                    elif kind == "route":
                        wr = cut(R("wr"), KT, 36)
                        out = wait_free(pe, (step, "lg"), l)
                        pe.wait_ge(affine_ready, l * (2 * KT) + 2 * KT)
                        pe.wait_ge(samples_ready, l * 2 + 2)
                        for k in range(KT):
                            last = mm(out[0:36, 0:TOK], wr[:, k, :], hT[:, k, :], k == 0, k == KT - 1)
                        made(last, (step, "lg"))
                        for j in range(6):
                            tt, half = j // 2, j % 2
                            rows = TTILES[tt][1]
                            if j == 2:
                                out = ps[bank((step, "lgt"))]
                                for t3, n in TTILES:
                                    last = transposed(out[0:n, t3 * 64:t3 * 64 + 36], lgs[0:36, t3 * P:t3 * P + n], C("ident")[0:36, 0:36])
                                made(last, (step, "lgt"))
                            if j == 1:
                                wait_free(pe, (step, "lgt"), l, [(step, "lg")])
                            out = wait_free(pe, (step, f"h{j}"), l)
                            for kk in range(4):
                                last = transposed(out[0:rows, kk * P:kk * P + P], hT[:, 4 * half + kk, tt * P:tt * P + rows], C("ident"))
                            made(last, (step, f"h{j}"))
                        pe.wait_ge(counts_ready, l * 3 + 1)
                        out = wait_free(pe, (step, "rk"), l)
                        mm(out[:, 0:NE], C("tri"), cnt[:, 0, :], True, True)
                        mm(out[:, NE:2 * NE], ones[:, :], cnt[:, 0, :], True, False)
                        mm(out[:, NE:2 * NE], C("tri"), cnt[:, 1, :], False, True)
                        mm(out[0:NS, 2 * NE:3 * NE], ones[:, 0:NS], cnt[:, 0, :], True, False)
                        mm(out[0:NS, 2 * NE:3 * NE], ones[:, 0:NS], cnt[:, 1, :], False, False)
                        made(mm(out[0:NS, 2 * NE:3 * NE], C("tri")[0:NS, 0:NS], cnt[0:NS, 2, :], False, True), (step, "rk"))
                        out = wait_free(pe, (step, "cnt"), l)
                        mm(out[0:NE, 0:1], cnt[:, 0, :], ones[:, 0:1], True, False)
                        mm(out[0:NE, 0:1], cnt[:, 1, :], ones[:, 0:1], False, False)
                        made(mm(out[0:NE, 0:1], cnt[0:NS, 2, :], ones[0:NS, 0:1], False, True), (step, "cnt"))
                        pe.wait_ge(counts_ready, l * 3 + 2)
                        out = wait_free(pe, (step, "ob"), l)
                        mm(out[:, 0:NE], nbb[0:NE, :], C("tri")[0:NE, 0:NE], True, True)
                        made(mm(out[:, NE:2 * NE], nbb[0:NE, :], C("tri_incl")[0:NE, 0:NE], True, True), (step, "ob"))
                        pe.wait_ge(counts_ready, l * 3 + 3)
                        for tt, rows in TTILES:
                            out = wait_free(pe, (step, f"bc{tt}"), l)
                            made(mm(cut(out[:, 0:4 * rows], 4, rows), ones[0:rows, :], diag[0:rows, 4 * tt:4 * tt + 4, 0:rows], True, True), (step, f"bc{tt}"))
                        pe.wait_ge(sel_ready, l * SELS + 1)
                        for half in range(2):
                            out = wait_free(pe, f"gather{half}", l, [(step, f"h{j}") for j in range(6)])
                            made(gather(out, half, 0), f"gather{half}")

                sel = cut(C("sel"), 2, 64)
                with pe.Fori(0, BODIES) as i:
                    for g in range(2):
                        for b in range(2):
                            pe.wait_ge(acc_free[b], l * LAYER_USES[b] + i * BODY_USES[b] + (TOKEN_USES[b] + g + 1))
                        for pair in range(2):
                            for q in range(2):
                                n = 6 * g + 3 * pair + q
                                e = 2 * pair + q
                                w = cut(mslot(n, l, i)[:, :], KT, 512)
                                if q == 0:
                                    out = mwait_free(pe, (g, f"gu{pair}"), l, i)
                                for k in range(KT):
                                    for j in range(4):
                                        last = mm(out[32 * j:32 * j + 32, q * P:q * P + P], hg[:, g, k, e * CAP:e * CAP + CAP],
                                                  w[:, k, j * P:j * P + P], k == 0, k == KT - 1, skip_group_check=True)
                                if q == 1:
                                    mmade(last, (g, f"gu{pair}"))
                                freed.append(n % RING)
                            name = (g, "ga" if pair == 0 else "gb")
                            gout = mwait_free(pe, name, l, i)
                            pe.wait_ge(sel_ready, l * SELS + i * 2 + (g + 2))
                            mmade(gather(gout, pair, 1 - g), name)
                            out = mwait_free(pe, (g, f"h{pair}"), l, i)
                            mwait_read(pe, (g, f"gu{pair}"), l, i)
                            for q in range(2):
                                for parity in range(2):
                                    last = mm(out[64 * parity:64 * parity + 64, q * 64:q * 64 + 64], hid[:, 2 * pair + q, :], sel[:, parity, :],
                                              True, True, skip_group_check=True)
                            mmade(last, (g, f"h{pair}"))
                            n = 6 * g + 3 * pair + 2
                            w = cut(mslot(n, l, i)[:, :], 2, 2, D)
                            mwait_read(pe, (g, f"h{pair}"), l, i)
                            for half in range(2):
                                out = ps[mbank((g, f"y{half}"))]
                                if pair == 0:
                                    mwait_free(pe, (g, f"y{half}"), l, i)
                                for ft in range(2):
                                    for q in range(2):
                                        e = 2 * pair + q
                                        at = (e * 2 + ft) * CAP
                                        last = mm(out[32 * e:32 * e + 32, :], hidT[:, at:at + CAP], w[:, q, ft, half * 512:half * 512 + 512],
                                                  ft == 0, ft == 1, skip_group_check=True)
                                if pair == 1:
                                    mmade(last, (g, f"y{half}"))
                            freed.append(n % RING)
                        pe.wait_ge(tables_ready, l + 1)
                        pe.wait_ge(pt_ready, l * GROUPS4 + i * 2 + (g + 1))
                        for half in range(2):
                            mwait_read(pe, (g, f"y{half}"), l, i)
                        for ft in range(KT):
                            out = mwait_free(pe, (g, f"c{ft}"), l, i)
                            for cols in ((slice(0, SEQ), SAMPLES) if ft == 0 else (slice(0, TOK),)):
                                last = mm(out[:, cols], yslot[:, ft * P:ft * P + P], pt[:, g, cols], True, True)
                            mmade(last, (g, f"c{ft}"))

                first = pe.value_load(novi[0:1, 0:1], min_val=0, max_val=DEPTH * NOVER)
                number = pe.value_load(novi[0:1, 1:2], min_val=0, max_val=NOVER)
                for b in range(8):
                    pe.wait_ge(acc_free[b], l * LAYER_USES[b] + LAYER_USES[b] + 1)
                pe.wait_ge(sel_ready, l * SELS + SELS)
                with pe.If(number > 0):
                    with pe.Fori(0, number) as n:
                        o = first + n
                        pe.wait_ge(over_sum_taken, o * KT + 1)
                        pe.wait_ge(over_rows_ready, o + 1)
                        pe.wait_ge(over_gu_loaded, o * 16 + 16)
                        w = cut(ovw, KT, 512)
                        for k in range(KT):
                            last = mm(ps[2][:, :], hg[:, 0, k, :], w[:, k, :], k == 0, k == KT - 1)
                        last.then_inc(over_gu_made, 1)
                        pe.wait_ge(over_sel_ready, o + 1)
                        gather(ps[0], 0, 1)
                        gather(ps[1], 1, 1).then_inc(over_gather_made, 1)
                        pe.wait_ge(over_hidden, o * TURNS + 3)
                        for f in range(2):
                            last = transposed(ps[3][:, f * P:f * P + P], hid[:, 2 * f:2 * f + 2, :].rearrange("p a b -> p (a b)"), C("ident"))
                        last.then_inc(over_hidden, 1)
                        pe.wait_ge(over_hidden, o * TURNS + 5)
                        pe.wait_ge(over_down_loaded, o * 16 + 16)
                        for half in range(2):
                            for f in range(2):
                                last = mm(ps[4 + half][:, :], hidT[:, f * P:f * P + P], ovd[:, f * D + half * 512:f * D + half * 512 + 512], f == 0, f == 1)
                        last.then_inc(over_down_made, 1)
                        pe.wait_ge(over_hidden, o * TURNS + TURNS + 1)
                        for ft in range(KT):
                            if ft >= len(SUM_BANKS):
                                pe.wait_ge(over_sum_taken, o * KT + (ft - len(SUM_BANKS) + 2))
                            out = ps[SUM_BANKS[ft % len(SUM_BANKS)]]
                            mm(out[:, 0:TOK], yslot[:, ft * P:ft * P + P], pt[:, 0, :], True, True).then_inc(over_sum_made, 1)
                pe.wait_ge(over_sum_taken, (first + number) * KT + 1)
                pe.wait_ge(over_rows_ready, (first + number) + 1)
            pe.wait_ge(square_ready, DEPTH * 2 + 1)
            pe.wait_ge(acc_free[FINAL_BANK], DEPTH * LAYER_USES[FINAL_BANK] + 1)
            for k in range(KT):
                last = mm(ps[FINAL_BANK][:, 0:TOK], ones[:, :], square[:, k, :], k == 0, k == KT - 1)
            last.then_inc(acc_ready[FINAL_BANK], 1)

        @block.scalar
        def _(act):
            def apply(out, in_, func, **k):
                return act.activation(out, in_, func, **k)

            def store_state(l, b):
                wait_read(act, (("st", b), f"1{HEADS - 1}"), l)
                r = SLOT_OF["st", b] % RING
                act.dma_start(row(state_sample_out, l * NB + b), ring[r][:, :]).then_inc(slot_free[r], 16)

            act.wait_ge(consts_loaded, 64)
            apply(cT[:, :, :], cT[:, :, :], ACT.Silu).then_inc(silu_c_ready, 1)
            with act.Fori(0, DEPTH) as l:
                n_var = 3
                for step in STEPS:
                    kind, i = step
                    if kind == "mod":
                        out = wait_made(act, (step, "modp"), l)
                        taken(apply(modp[:, i % 2, :], out[:, :], ACT.Copy), (step, "modp"))
                    elif kind == "norm":
                        act.wait_ge(x_ready, l * 2 + (i - 1))
                        apply(square, xT[:, :, :], ACT.Square).then_inc(square_ready, 1)
                        out = wait_made(act, (step, "ss"), l)
                        taken(apply(rms[:, :], out[:, 0:TOK], ACT.Sqrt, scale=1.0 / D, bias=C("eps")), (step, "ss"))
                        act.wait_ge(scaled_ready, l * 2 + i)
                        shift = 0 if i == 1 else 3 * KT
                        for k in range(KT):
                            apply(hT[:, k, 0:SEQ], hT[:, k, 0:SEQ], ACT.Identity, scale=scaled[:, k, 0:1],
                                  bias=mod[:, shift + k, 0:1]).then_inc(affine_ready, 1)
                    elif kind == "v":
                        for tt in range(2):
                            out = wait_made(act, (step, f"p{tt}"), l)
                            taken(apply(vn[:, tt, i * 512:i * 512 + 512], out[:, :], ACT.Gelu_apprx_tanh), (step, f"p{tt}"))
                        out = wait_made(act, (step, "s"), l)
                        taken(apply(vns[:, i, :], out[:, 0:P], ACT.Gelu_apprx_tanh), (step, "s"))
                    elif kind == "u":
                        for c in range(4):
                            out = wait_made(act, (step, f"c{c}"), l)
                            taken(apply(uT[:, 4 * i + c, :], out[:, 0:TOK], ACT.Gelu_apprx_tanh), (step, f"c{c}"))
                    elif kind in ("ga", "gb"):
                        dst = merged if kind == "ga" else sgb
                        for c in range(4):
                            out = wait_made(act, (step, f"c{c}"), l)
                            taken(apply(dst[:, 4 * i + c, :], out[:, 0:TOK], ACT.Sigmoid), (step, f"c{c}"))
                    elif kind in ("vr", "gr"):
                        if step == ("vr", 0):
                            act.wait_ge(v_stored, l * 16 + 16)
                        dst, dsts, func = (vr, vrs, ACT.Copy) if kind == "vr" else (sg, sgs, ACT.Silu)
                        for tt in range(2):
                            out = wait_made(act, (step, f"p{tt}"), l)
                            heads = cut(dst[:, tt, :], HEADS, DV)[:, :, i * P:i * P + P]
                            taken(apply(heads, cut(out[:, :], HEADS, P), func), (step, f"p{tt}"))
                        out = wait_made(act, (step, "s"), l)
                        taken(apply(dsts[:, i * P:i * P + P], out[:, 0:P], func), (step, "s"))
                    elif kind == "st" and i >= 1:
                        store_state(l, i - 1)
                    elif step == ("modflush", 9):
                        store_state(l, NB - 1)
                    elif kind == "kts":
                        out = wait_made(act, (step, "t"), l)
                        taken(apply(kzs[:, :], out[:, 0:DK], ACT.Copy), (step, "t"))
                    elif kind == "kt":
                        out = wait_made(act, (step, "t"), l)
                        taken(apply(kz[:, :, :], cut(out[:, :], 2, DK), ACT.Copy, scale=C("zeta")[:, i:i + 1]), (step, "t"))
                    elif kind in ("r1", "y"):
                        if kind == "r1":
                            if i >= 2:
                                act.wait_ge(rf_stored, l * (16 * HEADS) + 16 * (i - 1))
                            for dt in range(2):
                                out = wait_made(act, (step, f"r{dt}"), l)
                                taken(apply(r1[:, i % 2, dt, :], out[:, :], ACT.Copy), (step, f"r{dt}"))
                        c = 0 if kind == "r1" else 1
                        wait_read(act, (step, f"y{c}"), l)
                        act.wait_ge(rstd_ready, l * VARS + n_var + 1)
                        rows = sg[:, c, i * DV:i * DV + DV]
                        apply(rows, rows, ACT.Copy, scale=rstd[:, n_var % 2:n_var % 2 + 1]).then_inc(b_ready, 1)
                        n_var += 1
                    elif kind == "ysum":
                        wait_read(act, "ysample", l)
                        act.wait_ge(rstd_ready, l * VARS + n_var + 1)
                        apply(sgs, sgs, ACT.Copy, scale=rstd[:, n_var % 2:n_var % 2 + 1]).then_inc(b_ready, 1)
                        n_var += 1
                    elif kind == "bts":
                        out = wait_made(act, (step, "t"), l)
                        for c in range(4):
                            dst = bT.rearrange("p (h c) t -> p h c t", c=4)[:, :, c, SAMPLES]
                            last = apply(dst, cut(out[:, c * P:c * P + P], HEADS, NS), ACT.Copy)
                        taken(last, (step, "t"))
                    elif kind == "bt" and i % 2 == 0:
                        out = wait_made(act, (step, "t"), l)
                        tt, q = i // 4, i % 4
                        taken(apply(bT[:, 4 * q:4 * q + 4, tt * P:tt * P + P], cut(out[:, :], 4, P), ACT.Copy), (step, "t"))
                    elif kind == "route":
                        out = wait_made(act, (step, "lg"), l)
                        taken(apply(lgs[0:36, :], out[0:36, 0:TOK], ACT.Identity, bias=R("br")[0:36, :]), (step, "lg"))
                        for j in range(6):
                            tt, half = j // 2, j % 2
                            rows = TTILES[tt][1]
                            out = wait_made(act, (step, f"h{j}"), l)
                            taken(apply(htok[0:rows, tt, half * 512:half * 512 + 512], out[0:rows, :], ACT.Copy), (step, f"h{j}"))
                        for n in range(2):
                            act.wait_ge(exp_in, l * 2 + n + 1)
                            if n == 0:
                                apply(eg, g4, ACT.Exp).then_inc(exp_out, 1)
                            else:
                                apply(col[:, 8, :], col[:, 7, :], ACT.Exp).then_inc(exp_out, 1)
                        for tt, rows in TTILES:
                            out = wait_made(act, (step, f"bc{tt}"), l)
                            taken(apply(rows4[:, :, tt * P:tt * P + rows], cut(out[:, 0:4 * rows], 4, rows), ACT.Copy), (step, f"bc{tt}"))
                        for half in range(2):
                            out = wait_made(act, f"gather{half}", l)
                            taken(apply(hg[:, 0, 4 * half:4 * half + 4, :], cut(out[:, :], 4, P), ACT.Copy), f"gather{half}")
                assert n_var == VARS

                def silu_gate(out, dst, experts):
                    gate = cut(out, experts, 2, 64)[:, :, 0, :]
                    return apply(dst, gate, ACT.Silu)

                with act.Fori(0, BODIES) as i:
                    for g in range(2):
                        for pair in range(2):
                            out = mwait_made(act, (g, f"gu{pair}"), l, i)
                            mwait_made(act, (1 - g, f"h{pair}"), l, i, back=1 - g)
                            silu_gate(out[:, 0:2 * P], hid[:, 2 * pair:2 * pair + 2, :], 2).then_inc(silu_ready, 1)
                            name = (g, "ga" if pair == 0 else "gb")
                            out = mwait_made(act, name, l, i)
                            mtaken(apply(hg[:, 1 - g, 4 * pair:4 * pair + 4, :], cut(out[:, :], 4, P), ACT.Copy), name)
                            out = mwait_made(act, (g, f"h{pair}"), l, i)
                            mtaken(apply(hidT[:, pair * P:pair * P + P], out[:, 0:P], ACT.Copy), (g, f"h{pair}"))
                        act.wait_ge(tables_ready, l + 1)
                        out = mwait_made(act, (g, "y0"), l, i)
                        mtaken(apply(yslot[:, 0:512], out[:, :], ACT.Copy), (g, "y0"))

                first = act.value_load(novi[0:1, 0:1], min_val=0, max_val=DEPTH * NOVER)
                number = act.value_load(novi[0:1, 1:2], min_val=0, max_val=NOVER)
                with act.If(number > 0):
                    with act.Fori(0, number) as n:
                        o = first + n
                        act.wait_ge(over_gu_made, o + 2)
                        silu_gate(ps[2][:, :], hid[:, :, :], 4).then_inc(over_hidden, 1)
                        act.wait_ge(over_hidden, o * TURNS + 4)
                        apply(hidT[:, :], ps[3][:, 0:2 * P], ACT.Copy).then_inc(over_hidden, 1)
                        act.wait_ge(over_down_made, o + 2)
                        apply(yslot[:, 0:512], ps[4][:, :], ACT.Copy).then_inc(over_hidden, 1)
                        act.wait_ge(over_gather_made, o + 1)
                        apply(hg[:, 0, 0:4, :], cut(ps[0][:, :], 4, P), ACT.Copy)
                        apply(hg[:, 0, 4:8, :], cut(ps[1][:, :], 4, P), ACT.Copy).then_inc(over_rows_ready, 1)
                act.nop()
            act.wait_ge(x_ready, DEPTH * 2)
            apply(square, xT[:, :, :], ACT.Square).then_inc(square_ready, 1)
            act.wait_ge(acc_ready[FINAL_BANK], DEPTH * LAYER_USES[FINAL_BANK] + 1)
            apply(rms[:, :], ps[FINAL_BANK][:, 0:TOK], ACT.Sqrt, scale=1.0 / D, bias=C("eps")).then_inc(rms_ready, 1)

        @block.vector
        def _(dve):
            def settle():
                dve.drain()

            def moments_of(parts, n, l):
                if n >= 2:
                    dve.wait_ge(rstd_ready, l * VARS + n - 1)
                for m, ap in enumerate(parts):
                    dve.bn_stats(stats[:, m, :], ap)
                settle()
                dve.bn_aggr(moments[:, n % 2, :], stats[:, 0:len(parts), :]).then_inc(var_ready, 1)

            def layer_norm(rows, n, l, gain, offset):
                dve.wait_ge(rstd_ready, l * VARS + n + 1)
                m = n % 2
                dve.tensor_scalar(rows, rows, moments[:, m, 0:1], rstd[:, m:m + 1], ALU.subtract, ALU.mult)
                settle()
                dve.tensor_tensor(rows, rows, gain, ALU.mult)
                settle()
                dve.tensor_tensor(rows, rows, offset, ALU.add).then_inc(ln_ready, 1)

            def by_sequence(ap):
                return ap[:, :, SAMPLES].rearrange("p k (b t) -> p k b t", t=NT)

            def of_rows(ap):
                k = ap.shape[1]
                return ap[:, :, 1:ROWS].rearrange("p k (b o) -> p k b o", o=1).broadcast_to([P, k, NB, NT])

            def build_sel(buf, signal=None):
                for tt, rows in TTILES:
                    p = psel[0:rows, 3 * buf + tt, :]
                    dve.tensor_scalar(p, C("iota")[0:rows, :], vals[0:rows, tt, 0:1], None, ALU.is_equal)
                settle()
                for tt, rows in TTILES:
                    p = psel[0:rows, 3 * buf + tt, :]
                    last = dve.scalar_tensor_tensor(p, C("iota")[0:rows, :], vals[0:rows, tt, 1:2], p, ALU.is_equal, ALU.add)
                if signal is not None:
                    last.then_inc(signal, 1)
                settle()
                dve.tensor_scalar(vals[:, :, 0:2], vals[:, :, 0:2], float(P), None, ALU.subtract)
                settle()

            def build_pt(buf):
                dve.scalar_tensor_tensor(part, rows4[:, 0, :], slotcol[:, :], rows4[:, 2, :], ALU.is_equal, ALU.mult)
                dve.scalar_tensor_tensor(pt[:, buf, :], rows4[:, 1, :], slotcol[:, :], rows4[:, 3, :], ALU.is_equal, ALU.mult)
                settle()
                dve.tensor_scalar(slotcol[:, :], slotcol[:, :], float(P), None, ALU.add)
                return dve.tensor_tensor(pt[:, buf, :], pt[:, buf, :], part, ALU.add)

            def spread(ap, n):
                return ap.rearrange("p (t o) -> p t o", o=1).broadcast_to([ap.shape[0], ap.shape[1], n])

            def over_tokens(ap):
                return ap.rearrange("p (o n) -> p o n", o=1).broadcast_to([P, 3, ap.shape[1]])

            def first_largest(best, index, hot, values, work_, iota):
                n = iota.shape[1]
                dve.tensor_reduce(best, values, op=ALU.max, axis=AX.X)
                settle()
                dve.tensor_tensor(work_, values, spread(best, n), ALU.is_equal)
                settle()
                dve.tensor_tensor(work_, work_, over_tokens(iota), ALU.mult)
                settle()
                dve.tensor_reduce(index, work_, op=ALU.min, axis=AX.X)
                settle()
                dve.tensor_tensor(hot, over_tokens(iota), spread(index, n), ALU.is_equal)
                settle()

            def route(step, l):
                best, gi, gsum, gw, m1, i1, m2 = (col[:, n, :] for n in range(7))
                delta, ex, i2, den, e1, e2id = (col[:, n, :] for n in range(7, 13))
                dve.memset(rt[:, :, :], 0.0)
                dve.memset(slots[:, :, :], 0.0)
                settle()
                out = wait_made(dve, (step, "lgt"), l)
                dve.tensor_copy(rt[:, 0:2, :], cut(out[:, 0:128], 2, 64)[:, :, 0:36])
                taken(dve.tensor_copy(rt[0:NS, 2, :], out[0:NS, 128:164]), (step, "lgt"))
                settle()
                groups = rt[:, :, 0:GROUPS]
                first_largest(best, gi, g4b, groups, g4, C("iota4"))
                dve.tensor_tensor(g4, groups, spread(best, GROUPS), ALU.subtract).then_inc(exp_in, 1)
                experts = rt[:, :, GROUPS:36].rearrange("p t (g e) -> p t g e", g=GROUPS)
                hot = g4b.rearrange("p t (g o) -> p t g o", o=1).broadcast_to([P, 3, GROUPS, PER_GROUP])
                dve.tensor_tensor(prod.rearrange("p t (g e) -> p t g e", g=GROUPS), experts, hot, ALU.mult)
                settle()
                dve.tensor_reduce(ein, prod.rearrange("p t (g e) -> p t e g", g=GROUPS), op=ALU.add, axis=AX.X)
                settle()
                first_largest(m1, i1, oh8, ein, oh8b, C("iota8"))
                dve.scalar_tensor_tensor(e2, oh8, -3.0e38, ein, ALU.mult, ALU.add)
                settle()
                first_largest(m2, i2, oh8, e2, oh8b, C("iota8"))
                dve.tensor_tensor(delta, m2, m1, ALU.subtract).then_inc(exp_in, 1)
                dve.scalar_tensor_tensor(e1, gi, float(PER_GROUP), i1, ALU.mult, ALU.add)
                dve.scalar_tensor_tensor(e2id, gi, float(PER_GROUP), i2, ALU.mult, ALU.add)
                settle()
                dve.tensor_tensor(oh1, over_tokens(C("iota32")), spread(e1, NE), ALU.is_equal)
                dve.tensor_tensor(oh2, over_tokens(C("iota32")), spread(e2id, NE), ALU.is_equal)
                settle()
                dve.tensor_tensor(cnt, oh1, oh2, ALU.add).then_inc(counts_ready, 1)
                dve.wait_ge(exp_out, l * 2 + 1)
                dve.tensor_reduce(gsum, eg, op=ALU.add, axis=AX.X)
                settle()
                dve.reciprocal(gw, gsum)
                dve.wait_ge(exp_out, l * 2 + 2)
                dve.tensor_scalar(den, ex, 1.0, None, ALU.add)
                settle()
                dve.reciprocal(den, den)
                settle()
                dve.tensor_tensor(vals[:, :, 2], den, gw, ALU.mult)
                settle()
                dve.tensor_tensor(vals[:, :, 3], vals[:, :, 2], ex, ALU.mult)
                out = wait_made(dve, (step, "cnt"), l)
                dve.tensor_scalar(diff[0:NE, 0:1], out[0:NE, 0:1], float(CAP), None, ALU.is_gt)
                taken(dve.tensor_scalar(diff[0:NE, 1:2], out[0:NE, 0:1], float(CAP + OCAP), None, ALU.is_gt), (step, "cnt"))
                settle()
                dve.tensor_tensor(diff[0:NE, 2:3], diff[0:NE, 0:1], diff[0:NE, 1:2], ALU.add)
                settle()
                dve.tensor_copy(nbb[0:NE, :], diff[0:NE, 2:3].broadcast_to([NE, P])).then_inc(counts_ready, 1)
                settle()
                out = wait_made(dve, (step, "rk"), l)
                dve.tensor_copy(slots[:, 0:2, :], cut(out[:, 0:2 * NE], 2, NE))
                taken(dve.tensor_copy(slots[0:NS, 2, :], out[0:NS, 2 * NE:3 * NE]), (step, "rk"))
                out = wait_made(dve, (step, "ob"), l)
                taken(dve.tensor_copy(obe, cut(out[:, 0:2 * NE], 2, NE)), (step, "ob"))
                settle()
                dve.tensor_scalar(diff, obe[:, 0, :], float(OCAP), float(NE * CAP - CAP), ALU.mult, ALU.add)
                dve.tensor_scalar(picked, slots, float(CAP), None, ALU.is_ge)
                settle()
                dve.tensor_tensor(diff, diff, C("base32"), ALU.subtract)
                settle()
                dve.tensor_tensor(picked, picked, over_tokens(diff), ALU.mult)
                dve.tensor_tensor(slots, slots, over_tokens(C("base32")), ALU.add)
                settle()
                dve.tensor_tensor(slots, slots, picked, ALU.add)
                settle()
                for n, one in enumerate((oh1, oh2)):
                    dve.tensor_tensor(picked, slots, one, ALU.mult)
                    settle()
                    dve.tensor_reduce(vals[:, :, n], picked, op=ALU.add, axis=AX.X)
                    settle()
                for tt, rows in TTILES:
                    eye = C("ident")[0:rows, 0:rows].rearrange("p (o t) -> p o t", o=1).broadcast_to([rows, 4, rows])
                    last = dve.tensor_tensor(diag[0:rows, 4 * tt:4 * tt + 4, 0:rows], eye, spread(vals[0:rows, tt, :], rows), ALU.mult)
                last.then_inc(counts_ready, 1)
                wait_made(dve, (step, "h5"), l)
                dve.memset(hT[:, :, :], 0.0)
                dve.tensor_copy(slotcol[:, :], C("slotcol"))
                settle()
                build_sel(0, sel_ready)
                build_sel(1, sel_ready)
                def over_blocks(ap):
                    return ap.rearrange("p (o e) -> p o e", o=1).broadcast_to([1, NOVER, NE])

                number = C("novr")[0:1, :].rearrange("p (o e) -> p o e", e=1).broadcast_to([1, NOVER, NE])
                dve.tensor_tensor(ot1[0:1, :, :], over_blocks(obe[0:1, 0, :]), number, ALU.is_le)
                dve.tensor_tensor(ot2[0:1, :, :], over_blocks(obe[0:1, 1, :]), number, ALU.is_gt)
                settle()
                dve.tensor_tensor(ot1[0:1, :, :], ot1[0:1, :, :], ot2[0:1, :, :], ALU.mult)
                settle()
                for n, table in enumerate(("gurow", "drow", "dhalf")):
                    dve.tensor_tensor(ot2[0:1, :, :], ot1[0:1, :, :], over_blocks(C(table)[0:1, :]), ALU.mult)
                    settle()
                    dve.tensor_reduce(otf[0:1, n, :], ot2[0:1, :, :], op=ALU.add, axis=AX.X)
                    settle()
                dve.tensor_copy(otab[:, :, :], otf[0:1, :, :])
                dve.tensor_tensor(novf[:, 0:1], novf[:, 0:1], novf[:, 1:2], ALU.add)
                settle()
                dve.tensor_copy(novf[:, 1:2], obe[0:1, 1, NE - 1:NE])
                settle()
                dve.tensor_copy(novi[:, :], novf[:, :]).then_inc(tables_ready, 1)

            for b in range(8):
                dve.sem_inc(acc_free[b], 1)
            for s in (over_gu_made, over_hidden, over_down_made, over_sum_taken, over_rows_ready, over_sel_ready):
                dve.sem_inc(s, 1)
            dve.wait_ge(consts_loaded, 64)
            dve.wait_ge(setup_done, 2)
            with dve.Fori(0, DEPTH) as l:
                dve.wait_ge(params_loaded, l * 16 + 16)
                n_var = 3
                for step in STEPS:
                    kind, i = step
                    if kind in ("mod", "modflush"):
                        if kind == "mod" and i in (0, 4, 10):
                            continue
                        chunk = i - 1 if kind == "mod" else i
                        out = wait_made(dve, (step, "modt"), l)
                        parts = out[:, :].rearrange("p (f j r) -> p f r j", f=4, j=4)[:, :, 0:ROWS, :]
                        taken(dve.tensor_reduce(modsum[:, :, :], parts, op=ALU.add, axis=AX.X), (step, "modt"))
                        settle()
                        bias = R("bmod")[:, 4 * chunk:4 * chunk + 4].rearrange("p (f o) -> p f o", o=1).broadcast_to([P, 4, ROWS])
                        dve.tensor_tensor(mod[:, 4 * chunk:4 * chunk + 4, :], modsum[:, :, :], bias, ALU.add)
                        settle()
                    elif kind == "norm":
                        shift, scale, gain = (0, KT, "g1") if i == 1 else (3 * KT, 4 * KT, "g2")
                        gains = R(gain).rearrange("p (k o) -> p k o", o=1).broadcast_to([P, KT, ROWS])
                        dve.scalar_tensor_tensor(scaled[:, :, :], mod[:, scale:scale + KT, :], 1.0, gains, ALU.add, ALU.mult)
                        wait_read(dve, (step, "ss"), l)
                        dve.reciprocal(rms[:, :], rms[:, :])
                        settle()
                        each = rms[:, :].rearrange("p (o t) -> p o t", o=1).broadcast_to([P, KT, TOK])
                        dve.tensor_tensor(hT[:, :, :], xT[:, :, :], each, ALU.mult).then_inc(scaled_ready, 1)
                        settle()
                        hs = by_sequence(hT[:, :, :])
                        dve.tensor_tensor(hs, hs, of_rows(scaled[:, :, :]), ALU.mult)
                        settle()
                        dve.tensor_tensor(hs, hs, of_rows(mod[:, shift:shift + KT, :]), ALU.add).then_inc(samples_ready, 1)
                    elif step == ("v", 1):
                        for tt in range(2):
                            settle()
                            wait_reads(dve, [(("v", s), f"p{tt}") for s in range(2)], l)
                            moments_of([vn[:, tt, 0:512], vn[:, tt, 512:1024]], tt, l)
                        settle()
                        wait_reads(dve, [(("v", s), "s") for s in range(2)], l)
                        dve.bn_stats(stats[:, 0, :], work[:, VV_AT + 2 * D:VV_AT + 2 * D + 2 * P])
                        settle()
                        dve.bn_aggr(moments[:, 2, :], stats[:, 0:1, :]).then_inc(fold_ready, 1)
                        for tt in range(2):
                            layer_norm(vn[:, tt, :], tt, l, R("lng"), R("lnb"))
                    elif step == ("lnfold", 0):
                        out = wait_made(dve, (step, "t"), l)
                        taken(dve.tensor_copy(moments[:, 0, :], out[:, 0:2]), (step, "t"))
                        settle()
                        dve.tensor_tensor(moments[:, 3, 0:1], moments[:, 2, 0:1], moments[:, 0, 0:1], ALU.subtract)
                        settle()
                        dve.tensor_tensor(moments[:, 3, 1:2], moments[:, 3, 0:1], moments[:, 3, 0:1], ALU.mult).then_inc(fold_ready, 1)
                    elif step == ("lnfold", 1):
                        out = wait_made(dve, (step, "t"), l)
                        taken(dve.tensor_copy(moments[:, 3, :], out[:, 0:2]), (step, "t"))
                        settle()
                        dve.tensor_tensor(moments[:, 0, 1:2], moments[:, 0, 1:2], moments[:, 3, 1:2], ALU.add).then_inc(var_ready, 1)
                        layer_norm(work[:, VV_AT + 2 * D:VV_AT + 2 * D + 2 * P], 2, l, R("lngs"), R("lnbs"))
                    elif kind == "mix":
                        if i == 0:
                            wait_reads(dve, [(("u", s), f"c{c}") for s in range(2) for c in range(4)], l)
                        c, g = i // 2, 4 * (i % 2)
                        out = wait_made(dve, (step, "t"), l)
                        dve.tensor_tensor(mixed, out[:, :], R("bs")[:, g * P:g * P + 512], ALU.add)
                        settle()
                        us = uT[:, g:g + 4, c * P:c * P + P]
                        taken(dve.tensor_tensor(us, us, cut(mixed, 4, P), ALU.mult), (step, "t"))
                        settle()
                    elif kind == "mixs":
                        out = wait_made(dve, (step, "t"), l)
                        pair = cut(mixed[:, 0:2 * NS], 2, NS)
                        bias = R("bss").rearrange("p (s j t) -> p s j t", s=2, j=4)[:, :, i, :]
                        dve.tensor_tensor(pair, cut(out[:, 0:2 * NS], 2, NS), bias, ALU.add)
                        settle()
                        us = uT.rearrange("p (s j) t -> p s j t", s=2)[:, :, i, SAMPLES]
                        taken(dve.tensor_tensor(us, us, pair, ALU.mult), (step, "t"))
                        settle()
                    elif kind == "a":
                        for c in range(4):
                            out = wait_made(dve, (step, f"c{c}"), l)
                            m = merged[:, 4 * i + c, :]
                            if i == 0 and c == 0:
                                wait_reads(dve, [(("ga", s), f"c{cc}") for s in range(2) for cc in range(4)], l)
                            taken(dve.tensor_tensor(m, m, out[:, 0:TOK], ALU.mult), (step, f"c{c}"))
                    elif kind in ("q", "k"):
                        dst = qT if kind == "q" else kT
                        for pair in range(2):
                            h = 2 * i + pair
                            x1 = wait_made(dve, (step, f"c{2 * pair}"), l)[:, 0:TOK]
                            x2 = wait_made(dve, (step, f"c{2 * pair + 1}"), l)[:, 0:TOK]
                            y1, y2 = dst[:, 2 * h, :], dst[:, 2 * h + 1, :]
                            dve.tensor_tensor(y1, x1, C("cos"), ALU.mult)
                            dve.tensor_tensor(y2, x1, C("sin"), ALU.mult)
                            dve.tensor_tensor(rope[:, 0, :], x2, C("sin"), ALU.mult)
                            dve.tensor_tensor(rope[:, 1, :], x2, C("cos"), ALU.mult)
                            settle()
                            taken(dve.tensor_tensor(y1, y1, rope[:, 0, :], ALU.subtract), (step, f"c{2 * pair}"))
                            taken(dve.tensor_tensor(y2, y2, rope[:, 1, :], ALU.add), (step, f"c{2 * pair + 1}"))
                            settle()
                    elif kind == "scs":
                        dve.wait_ge(qm_zero, l + 1)
                        xis = C("xis").rearrange("p (m b t) -> p m b t", m=KT, b=NB)
                        for b in range(NB):
                            last = dve.tensor_tensor(qm[:, b, :, NT * b:NT * b + NT], qT[:, :, SEQ + NT * b:SEQ + NT * b + NT], xis[:, :, b, :], ALU.mult)
                        last.then_inc(qm_ready, 1)
                        out = wait_made(dve, (step, "t"), l)
                        each = out[:, 0:NS].rearrange("p (o t) -> p o t", o=1).broadcast_to([P, HEADS, NS])
                        taken(dve.tensor_tensor(cut(scs[:, :], HEADS, NS), each, cut(C("masks"), HEADS, NS), ALU.mult), (step, "t"))
                    elif kind == "sc":
                        out = wait_made(dve, (step, "t"), l)
                        mask = C("decay")[:, i * P:i * P + P].rearrange("p (o t) -> p o t", o=1).broadcast_to([P, 2, P])
                        taken(dve.tensor_tensor(scT[:, :, :], cut(out[:, 0:2 * P], 2, P), mask, ALU.mult), (step, "t"))
                        xi = C("xi")[:, i * P:i * P + P].rearrange("p (o t) -> p o t", o=1).broadcast_to([P, 2, P])
                        dve.tensor_tensor(qx[:, :, :], qT[:, 2 * i:2 * i + 2, P:2 * P], xi, ALU.mult).then_inc(qx_ready, 1)
                    elif kind in ("r1", "y"):
                        c = 0 if kind == "r1" else 1
                        name = (step, f"y{c}")
                        settle()
                        out = wait_made(dve, name, l)
                        moments_of([out[:, :]], n_var, l)
                        settle()
                        rows = sg[:, c, i * DV:i * DV + DV]
                        if step == ("r1", 0):
                            wait_reads(dve, [(("gr", n), t) for n in range(4) for t in ("p0", "p1")], l)
                        taken(dve.scalar_tensor_tensor(rows, out[:, :], moments[:, n_var % 2, 0:1], rows, ALU.subtract, ALU.mult), name)
                        n_var += 1
                        if kind == "y":
                            for dt in range(2):
                                out = wait_made(dve, (step, f"f{dt}"), l)
                                r = r1[:, i % 2, dt, :]
                                taken(dve.scalar_tensor_tensor(r, r, math.exp(decay(i) * P), out[:, :], ALU.mult, ALU.add), (step, f"f{dt}"))
                    elif kind == "st":
                        state = cut(ring[SLOT_OF[step] % RING][:, :], HEADS, 2, DV)
                        for dt in range(2):
                            for h in range(HEADS):
                                name = (step, f"{dt}{h}")
                                out = wait_made(dve, name, l)
                                taken(dve.scalar_tensor_tensor(state[:, h, dt, :], state[:, h, dt, :], math.exp(decay(h) * NT), out[:, :], ALU.mult, ALU.add), name)
                    elif kind == "ysum":
                        settle()
                        out = wait_made(dve, "ysample", l)
                        moments_of([out[:, :]], n_var, l)
                        settle()
                        wait_reads(dve, [(("gr", n), "s") for n in range(4)], l)
                        taken(dve.scalar_tensor_tensor(sgs, out[:, :], moments[:, n_var % 2, 0:1], sgs, ALU.subtract, ALU.mult), "ysample")
                        n_var += 1
                    elif kind == "bt" and i % 2 == 1:
                        out = wait_made(dve, (step, "t"), l)
                        tt, q = i // 4, i % 4
                        taken(dve.tensor_copy(bT[:, 4 * q:4 * q + 4, tt * P:tt * P + P], cut(out[:, :], 4, P)), (step, "t"))
                    elif kind == "b":
                        for c in range(2):
                            f = 2 * i + c
                            if f == 0:
                                wait_reads(dve, [(("gb", s), f"c{cc}") for s in range(2) for cc in range(4)], l)
                            out = wait_made(dve, (step, f"c{c}"), l)
                            dve.tensor_tensor(rope[:, f % 2, :], out[:, 0:TOK], sgb[:, f, :], ALU.mult)
                            settle()
                            taken(dve.tensor_tensor(merged[:, f, :], merged[:, f, :], rope[:, f % 2, :], ALU.add), (step, f"c{c}"))
                    elif kind == "o":
                        for c in range(4):
                            f = 4 * i + c
                            out = wait_made(dve, (step, f"c{c}"), l)
                            dve.scalar_tensor_tensor(xT[:, f, 0:SEQ], out[:, 0:SEQ], mod[:, 2 * KT + f, 0:1], xT[:, f, 0:SEQ], ALU.mult, ALU.add)
                            part_s = rope[:, f % 2, 0:NS]
                            gate = of_rows(mod[:, 2 * KT + f:2 * KT + f + 1, :])[:, 0, :, :]
                            taken(dve.tensor_tensor(cut(part_s, NB, NT), cut(out[:, SAMPLES], NB, NT), gate, ALU.mult), (step, f"c{c}"))
                            settle()
                            last = dve.tensor_tensor(xT[:, f, SAMPLES], xT[:, f, SAMPLES], part_s, ALU.add)
                        if i == 1:
                            last.then_inc(x_ready, 1)
                    elif kind == "route":
                        route(step, l)
                assert n_var == VARS

                with dve.Fori(0, BODIES) as i:
                    for g in range(2):
                        for pair in range(2):
                            name = (g, f"gu{pair}")
                            mwait_made(dve, name, l, i)
                            dve.wait_ge(silu_ready, l * (NE // 2) + i * 4 + (2 * g + pair + 1))
                            h = hid[:, 2 * pair:2 * pair + 2, :]
                            up = cut(ps[mbank(name)][:, 0:2 * P], 2, 2, 64)[:, :, 1, :]
                            mtaken(dve.tensor_tensor(h, h, up, ALU.mult), name)
                            if pair == 0:
                                mwait_made(dve, (g, f"c{KT - 1}"), l, i, back=1)
                                build_pt(g).then_inc(pt_ready, 1)
                        out = mwait_made(dve, (g, "y1"), l, i)
                        mtaken(dve.tensor_copy(yslot[:, 512:1024], out[:, :]), (g, "y1"))
                        build_sel(g, sel_ready)
                        for ft in range(KT):
                            out = mwait_made(dve, (g, f"c{ft}"), l, i)
                            mtaken(dve.tensor_tensor(hT[:, ft, :], hT[:, ft, :], out[:, 0:TOK], ALU.add), (g, f"c{ft}"))

                first = dve.value_load(novi[0:1, 0:1], min_val=0, max_val=DEPTH * NOVER)
                number = dve.value_load(novi[0:1, 1:2], min_val=0, max_val=NOVER)
                with dve.If(number > 0):
                    with dve.Fori(0, number) as n:
                        o = first + n
                        dve.wait_ge(over_hidden, o * TURNS + 2)
                        up = cut(ps[2][:, :], 4, 2, 64)[:, :, 1, :]
                        dve.tensor_tensor(hid[:, :, :], hid[:, :, :], up, ALU.mult).then_inc(over_hidden, 1)
                        build_pt(0)
                        settle()
                        dve.wait_ge(over_down_made, o + 2)
                        dve.tensor_copy(yslot[:, 512:1024], ps[5][:, :]).then_inc(over_hidden, 1)
                        for ft in range(KT):
                            dve.wait_ge(over_sum_made, o * KT + (ft + 1))
                            out = ps[SUM_BANKS[ft % len(SUM_BANKS)]]
                            dve.tensor_tensor(hT[:, ft, :], hT[:, ft, :], out[:, 0:TOK], ALU.add).then_inc(over_sum_taken, 1)
                        dve.wait_ge(over_gather_made, o + 1)
                        build_sel(1, over_sel_ready)
                settle()
                for k in range(KT):
                    dve.scalar_tensor_tensor(xT[:, k, 0:SEQ], hT[:, k, 0:SEQ], mod[:, 5 * KT + k, 0:1], xT[:, k, 0:SEQ], ALU.mult, ALU.add)
                hs, xs = by_sequence(hT[:, :, :]), by_sequence(xT[:, :, :])
                dve.tensor_tensor(hs, hs, of_rows(mod[:, 5 * KT:6 * KT, :]), ALU.mult)
                settle()
                dve.tensor_tensor(xs, xs, hs, ALU.add).then_inc(x_ready, 1)

            dve.wait_ge(rms_ready, 1)
            dve.reciprocal(rms[:, :], rms[:, :])
            settle()
            each = rms[:, :].rearrange("p (o t) -> p o t", o=1).broadcast_to([P, KT, TOK])
            dve.tensor_tensor(hT[:, :, :], xT[:, :, :], each, ALU.mult)
            settle()
            gains = gfs[:, :].rearrange("p (k o) -> p k o", o=1).broadcast_to([P, KT, TOK])
            dve.tensor_tensor(hT[:, :, :], hT[:, :, :], gains, ALU.mult).then_inc(x_ready, 1)


def kernel(**inputs):
    import concourse.bacc as bacc
    from concourse.bass_utils import run_bass_kernel_spmd

    a = {k: np.asarray(v) for k, v in inputs.items()}
    f = a["x_prompt"].dtype

    def feature_major(x):
        return np.ascontiguousarray(x.reshape(-1, KT, P).transpose(2, 1, 0))

    stream = np.zeros((DEPTH, LAYER_SLOTS, P, SLOT), f)

    def k_tiles(w):
        return w.reshape(-1, P, w.shape[1]).transpose(1, 0, 2).reshape(P, -1)

    sizes = [("u", D), ("v", D), ("q", QKW), ("k", QKW), ("vr", VW), ("gr", VW), ("ga", D), ("gb", D)]
    starts, at = {}, 0
    for name, width in sizes:
        starts[name] = at
        at += width
    for l in range(DEPTH):
        for (kind, i), n in SLOT_OF.items():
            if kind == "mod":
                block = k_tiles(a["w_mod"][l][:, i * 512:i * 512 + 512])
            elif kind in ("vr", "gr"):
                w = a["w_in"][l][:, starts[kind]:starts[kind] + VW].reshape(D, HEADS, DV)
                block = k_tiles(w[:, :, i * P:i * P + P].reshape(D, 512))
            elif kind in starts:
                at = starts[kind] + i * 512
                block = k_tiles(a["w_in"][l][:, at:at + 512])
            elif kind == "a":
                block = k_tiles(a["w_a_out"][l][:, i * 512:i * 512 + 512])
            elif kind == "b":
                block = k_tiles(a["w_b_out"][l][:, i * 256:i * 256 + 256])
            elif kind == "o":
                block = k_tiles(a["w_o"][l][:, i * 512:i * 512 + 512])
            else:
                block = a["state_ret"][l, i].reshape(HEADS, 2, P, DV).transpose(2, 0, 1, 3).reshape(P, SLOT)
            stream[l, n] = block
        for e in range(NE):
            gate = a["w_gate"][l, e].reshape(D, 4, 1, 64)
            up = a["w_up"][l, e].reshape(D, 4, 1, 64)
            stream[l, TOKEN_SLOTS + e // 2 * 3 + e % 2] = k_tiles(np.concatenate([gate, up], axis=2).reshape(D, 512))
            half = stream[l, TOKEN_SLOTS + e // 2 * 3 + 2][:, e % 2 * 2 * D:(e % 2 + 1) * 2 * D]
            half[:] = k_tiles(a["w_down"][l, e])
    stream = stream.reshape(DEPTH * LAYER_SLOTS, P, SLOT)

    params = np.zeros((DEPTH + 1, P, PW), f)

    def every(x):
        return np.broadcast_to(x.reshape(1, -1), (P, x.size))

    for ll in range(DEPTH + 1):
        l = min(ll, DEPTH - 1)

        def put(name, value):
            at, width = PARAMS[name]
            params[ll][:, at:at + width] = value.reshape(P, width)

        def by_quarter(x):
            return np.broadcast_to(x.reshape(2, 4, P).transpose(1, 0, 2)[:, None], (4, NS, 2, P))

        put("bmod", a["b_mod"][l].reshape(6 * KT, P).T)
        put("g1", a["norm1_g"][l].reshape(KT, P).T)
        put("g2", a["norm2_g"][l].reshape(KT, P).T)
        put("lng", every(a["ln_v_g"][l]))
        put("lnb", every(a["ln_v_b"][l]))
        put("lngs", by_quarter(a["ln_v_g"][l]))
        put("lnbs", by_quarter(a["ln_v_b"][l]))
        put("bs", every(a["b_s"][l]))
        put("bss", every(np.tile(a["b_s"][l][:, :NT], (1, NB))))
        put("wst", a["w_s"][l].transpose(2, 0, 1))
        corner = a["w_s"][l][:, :NT, :NT].transpose(2, 0, 1).reshape(NT, 2, 4, NT)
        put("wss", np.broadcast_to(corner.transpose(2, 0, 1, 3)[:, None, :, :, None, :], (4, NB, NT, 2, NB, NT)))
        router = np.concatenate([a["w_router_group"][l], a["w_router_expert"][l]], axis=1)
        put("wr", k_tiles(router))
        params[ll][:GROUPS, PARAMS["br"][0]] = a["b_router_group"][l]
        params[ll][GROUPS:GROUPS + NE, PARAMS["br"][0]] = a["b_router_expert"][l]

    x = np.concatenate([a["x_prompt"].reshape(SEQ, D), a["x_sample"].reshape(NS, D)])
    c = np.zeros((P, KT, 32), f)
    c[:, :, :ROWS] = feature_major(np.concatenate([a["c_prompt"], a["c_sample"]]))
    arrays = {
        "stream": stream, "consts": constants(), "params": params, "x_in": feature_major(x), "c_in": c,
        "gfin": np.ascontiguousarray(a["final_g"].reshape(KT, P).T),
    }
    outs = {
        "y_out": (P, KT, TOK), "state_out": (DEPTH * HEADS, P, 2 * DV),
        "state_sample_out": (DEPTH * NB, P, SLOT), "v_out": (DEPTH, P, 2 * P),
    }
    nc = bacc.Bacc("TRN2", target_bir_lowering=False, num_devices=1)
    args = [nc.dram_tensor(n, v.shape, mybir.dt.from_np(v.dtype), kind="ExternalInput").ap() for n, v in arrays.items()]
    args += [nc.dram_tensor(n, s, mybir.dt.from_np(np.dtype(f)), kind="ExternalOutput").ap() for n, s in outs.items()]
    build(nc, *args)
    r = run_bass_kernel_spmd(nc, [arrays], core_ids=[0]).results[0]
    y = np.asarray(r["y_out"]).transpose(2, 1, 0).reshape(TOK, D)
    state = np.asarray(r["state_out"]).reshape(DEPTH, 1, HEADS, P, 2, DV).transpose(0, 1, 2, 4, 3, 5)
    state_sample = np.asarray(r["state_sample_out"]).reshape(DEPTH, NB, P, HEADS, 2, DV).transpose(0, 1, 3, 4, 2, 5)
    v = np.asarray(r["v_out"]).reshape(DEPTH, 4, NB, NT, 2, P).transpose(0, 2, 3, 4, 1, 5)
    return (
        np.ascontiguousarray(y[:SEQ]).reshape(1, SEQ, D),
        np.ascontiguousarray(y[SEQ:]).reshape(NB, NT, D),
        np.ascontiguousarray(state).reshape(DEPTH, 1, HEADS, DK, DV),
        np.ascontiguousarray(state_sample).reshape(DEPTH, NB, HEADS, DK, DV),
        np.ascontiguousarray(v).reshape(DEPTH, NB, NT, D),
    )
```
